# Optimizing a Trainium2 kernel written in Bass

```python
import math
import jax, jax.numpy as jnp
from jax import lax
import numpy as np

D_MODEL = 2048
BATCH = 1
SEQ = 256
DEPTH = 2

N_A_LAYERS = DEPTH // 2
N_B_LAYERS = DEPTH - N_A_LAYERS
RMS_EPS = 1e-6
L2_EPS = 1e-6
NEG_INF = -1e30
FORCE_SCORE = 1e4

GDN_QK_HEADS = 16
GDN_V_HEADS = 32
GDN_HEAD_DIM = 128
GDN_QK_DIM = GDN_QK_HEADS * GDN_HEAD_DIM
GDN_V_DIM = GDN_V_HEADS * GDN_HEAD_DIM
GDN_CONV_DIM = 2 * GDN_QK_DIM + GDN_V_DIM
GDN_CONV = 4
GDN_CHUNK = 64
GDN_IN_DIM = GDN_CONV_DIM + GDN_V_DIM + 2 * GDN_V_HEADS

NSA_HEADS = 16
NSA_KV_GROUPS = 4
NSA_HEADS_PER_GROUP = NSA_HEADS // NSA_KV_GROUPS
NSA_HEAD_DIM = 128
NSA_Q_DIM = NSA_HEADS * NSA_HEAD_DIM
NSA_IN_DIM = NSA_Q_DIM + 3 * NSA_HEADS
NSA_KV_DIM = 6 * NSA_KV_GROUPS * NSA_HEAD_DIM
CMP_BLOCK = 32
CMP_STRIDE = 16
CMP_HIDDEN = 256
SEL_BLOCK = 64
SEL_COUNT = 16
WINDOW = 512
Q_BLOCK = 128
SEL_RATIO = SEL_BLOCK // CMP_STRIDE
SEL_OVERLAP_W = (1.0, 2.0, 2.0, 2.0, 1.0)

FFN_HIDDEN = -(-8 * D_MODEL // (3 * 256)) * 256

kernel_name = "yoco_gdn_nsa_hybrid"

def rms_norm(x, g):
    xf = x.astype(jnp.float32)
    y = xf * lax.rsqrt(jnp.mean(xf * xf, axis=-1, keepdims=True) + RMS_EPS)
    return (y * g.astype(jnp.float32)).astype(x.dtype)

def l2_normalize(x):
    xf = x.astype(jnp.float32)
    return xf * lax.rsqrt(jnp.sum(xf * xf, axis=-1, keepdims=True) + L2_EPS)

def alibi_slopes(n):
    return 2.0 ** (-8.0 * jnp.arange(1, n + 1, dtype=jnp.float32) / n)

def swiglu_ffn(x, w_gate_up, w_down):
    gate, up = jnp.split(x @ w_gate_up, 2, axis=-1)
    return (jax.nn.silu(gate) * up) @ w_down

def causal_depthwise_conv(x, w):
    c = x.shape[-1]
    return lax.conv_general_dilated(
        x, w[:, None, :], window_strides=(1,), padding=[(w.shape[0] - 1, 0)],
        dimension_numbers=('NWC', 'WIO', 'NWC'), feature_group_count=c)

def chunk_gated_delta_rule(q, k, v, g, beta):
    B, T, H, Dk = q.shape
    Dv = v.shape[-1]
    C = GDN_CHUNK
    nc = T // C

    def to_chunks(a):
        a = jnp.moveaxis(a, 2, 1)
        return a.reshape(B, H, nc, C, *a.shape[3:])

    q = to_chunks(q) * (Dk ** -0.5)
    k, v, g, beta = to_chunks(k), to_chunks(v), to_chunks(g), to_chunks(beta)
    g_cum = jnp.cumsum(g, axis=-1)
    causal = jnp.tril(jnp.ones((C, C), dtype=bool))
    strict = jnp.tril(jnp.ones((C, C), dtype=bool), -1)
    decay = jnp.exp(jnp.where(causal, g_cum[..., :, None] - g_cum[..., None, :], -jnp.inf))
    k_beta = k * beta[..., None]
    l_mat = jnp.where(strict, jnp.einsum('bhnid,bhnjd->bhnij', k_beta, k) * decay, 0.0)
    rhs = jnp.concatenate([v * beta[..., None], k_beta * jnp.exp(g_cum)[..., None]], axis=-1)
    sol = lax.linalg.triangular_solve(l_mat, rhs, left_side=True, lower=True, unit_diagonal=True)
    u, w = sol[..., :Dv], sol[..., Dv:]
    attn_qk = jnp.einsum('bhnid,bhnjd->bhnij', q, k) * decay
    q_dec = q * jnp.exp(g_cum)[..., None]
    g_last = g_cum[..., -1]
    k_dec = k * jnp.exp(g_last[..., None] - g_cum)[..., None]
    xs = (jnp.moveaxis(q_dec, 2, 0), jnp.moveaxis(attn_qk, 2, 0), jnp.moveaxis(u, 2, 0),
          jnp.moveaxis(w, 2, 0), jnp.moveaxis(k_dec, 2, 0), jnp.moveaxis(g_last, 2, 0))

    def step(state, inp):
        q_c, a_c, u_c, w_c, k_c, gl = inp
        v_new = u_c - jnp.einsum('bhck,bhkv->bhcv', w_c, state)
        o_c = jnp.einsum('bhck,bhkv->bhcv', q_c, state) + jnp.einsum('bhij,bhjv->bhiv', a_c, v_new)
        state = state * jnp.exp(gl)[..., None, None] + jnp.einsum('bhck,bhcv->bhkv', k_c, v_new)
        return state, o_c

    state0 = jnp.zeros((B, H, Dk, Dv), jnp.float32)
    _, o = lax.scan(step, state0, xs)
    o = jnp.moveaxis(o, 0, 2).reshape(B, H, T, Dv)
    return jnp.moveaxis(o, 1, 2)

def gated_deltanet(x, w_in, conv_w, a_log, dt_bias, out_norm_g, w_out):
    B, T, _ = x.shape
    f32 = jnp.float32
    proj = x @ w_in
    qkv, z, b_raw, a_raw = jnp.split(
        proj, [GDN_CONV_DIM, GDN_CONV_DIM + GDN_V_DIM, GDN_CONV_DIM + GDN_V_DIM + GDN_V_HEADS], axis=-1)
    qkv = jax.nn.silu(causal_depthwise_conv(qkv, conv_w))
    q, k, v = jnp.split(qkv, [GDN_QK_DIM, 2 * GDN_QK_DIM], axis=-1)
    rep = GDN_V_HEADS // GDN_QK_HEADS
    q = jnp.repeat(l2_normalize(q.reshape(B, T, GDN_QK_HEADS, GDN_HEAD_DIM)), rep, axis=2)
    k = jnp.repeat(l2_normalize(k.reshape(B, T, GDN_QK_HEADS, GDN_HEAD_DIM)), rep, axis=2)
    v = v.reshape(B, T, GDN_V_HEADS, GDN_HEAD_DIM).astype(f32)
    beta = jax.nn.sigmoid(b_raw.astype(f32))
    g = -jnp.exp(a_log.astype(f32)) * jax.nn.softplus(a_raw.astype(f32) + dt_bias.astype(f32))
    o = chunk_gated_delta_rule(q, k, v, g, beta)
    o = rms_norm(o, out_norm_g) * jax.nn.silu(z.reshape(B, T, GDN_V_HEADS, GDN_HEAD_DIM).astype(f32))
    return o.reshape(B, T, GDN_V_DIM).astype(x.dtype) @ w_out

def compress_blocks(x_tok, pos, w1, w2):
    B, G, T, D = x_tok.shape
    seg = x_tok.reshape(B, G, T // CMP_STRIDE, CMP_STRIDE, D)
    blocks = jnp.concatenate([seg[:, :, :-1], seg[:, :, 1:]], axis=3)
    blocks = (blocks + pos).reshape(B, G, blocks.shape[2], CMP_BLOCK * D)
    return jax.nn.silu(blocks @ w1) @ w2

def nsa_shared_kv(h, kv_norm_g, kv_w, cmp_pos, cmp_w1_k, cmp_w2_k, cmp_w1_v, cmp_w2_v):
    B, T, _ = h.shape
    kv = (rms_norm(h, kv_norm_g) @ kv_w).reshape(B, T, 6, NSA_KV_GROUPS, NSA_HEAD_DIM)
    kv = jnp.transpose(kv, (2, 0, 3, 1, 4))
    k_cmp = compress_blocks(kv[0], cmp_pos, cmp_w1_k, cmp_w2_k)
    v_cmp = compress_blocks(kv[1], cmp_pos, cmp_w1_v, cmp_w2_v)
    nsb = T // SEL_BLOCK
    k_slc = kv[2].reshape(B, NSA_KV_GROUPS, nsb, SEL_BLOCK, NSA_HEAD_DIM)
    v_slc = kv[3].reshape(B, NSA_KV_GROUPS, nsb, SEL_BLOCK, NSA_HEAD_DIM)
    pad = ((0, 0), (0, 0), (WINDOW, 0), (0, 0))
    k_win = jnp.pad(kv[4], pad)
    v_win = jnp.pad(kv[5], pad)
    return (k_cmp, v_cmp, k_slc, v_slc, k_win, v_win)

def nsa_attention(x, shared_kv, w_in, w_out):
    k_cmp, v_cmp, k_slc, v_slc, k_win, v_win = shared_kv
    B, T, _ = x.shape
    G, HG, D = NSA_KV_GROUPS, NSA_HEADS_PER_GROUP, NSA_HEAD_DIM
    f32 = jnp.float32
    nqb = T // Q_BLOCK
    ncb = k_cmp.shape[2]
    nsb = k_slc.shape[2]
    n_sel = min(SEL_COUNT, nsb)
    proj = x @ w_in
    q = proj[..., :NSA_Q_DIM] * (D ** -0.5)
    q = jnp.transpose(q.reshape(B, nqb, Q_BLOCK, G, HG, D), (1, 0, 3, 4, 2, 5))
    gates = jax.nn.sigmoid(proj[..., NSA_Q_DIM:].astype(f32))
    gates = jnp.transpose(gates.reshape(B, nqb, Q_BLOCK, 3, G, HG), (1, 3, 0, 4, 5, 2))
    starts = jnp.arange(nqb, dtype=jnp.int32) * Q_BLOCK

    slopes = alibi_slopes(NSA_HEADS).reshape(1, G, HG, 1, 1)
    cmp_idx = jnp.arange(ncb, dtype=jnp.int32)
    cmp_end = cmp_idx * CMP_STRIDE + (CMP_BLOCK - 1)
    cmp_centre = cmp_idx.astype(f32) * CMP_STRIDE + (CMP_BLOCK - 1) / 2
    blk = jnp.arange(nsb, dtype=jnp.int32)
    b_ix = jnp.arange(B)[:, None, None, None]
    g_ix = jnp.arange(G)[None, :, None, None]

    def query_block(args):
        qb, gb, start = args
        t = start + jnp.arange(Q_BLOCK, dtype=jnp.int32)
        tf = t.astype(f32)
        valid_c = cmp_end[None, :] <= t[:, None]
        s_c = jnp.einsum('bghqd,bgnd->bghqn', qb, k_cmp, preferred_element_type=f32)
        s_c = s_c - slopes * (tf[:, None] - cmp_centre[None, :])
        p_c = jnp.where(valid_c, jax.nn.softmax(jnp.where(valid_c, s_c, NEG_INF), axis=-1), 0.0)
        o_cmp = jnp.einsum('bghqn,bgnd->bghqd', p_c.astype(v_cmp.dtype), v_cmp)
        imp = jnp.pad(p_c.sum(axis=2), ((0, 0), (0, 0), (0, 0), (1, SEL_RATIO * nsb + SEL_RATIO - 1 - ncb)))
        imp_slc = sum(wt * imp[..., o:o + SEL_RATIO * nsb:SEL_RATIO] for o, wt in enumerate(SEL_OVERLAP_W))
        cur = t // SEL_BLOCK
        forced = (blk[None, :] == 0) | (blk[None, :] == cur[:, None]) | (blk[None, :] == cur[:, None] - 1)
        visible = blk[None, :] * SEL_BLOCK <= t[:, None]
        score = jnp.where(visible, jnp.where(forced, FORCE_SCORE, imp_slc), NEG_INF)
        _, sel = lax.top_k(score, n_sel)
        k_sel = k_slc[b_ix, g_ix, sel]
        v_sel = v_slc[b_ix, g_ix, sel]
        dist_s = t[:, None, None] - (sel[..., None] * SEL_BLOCK + jnp.arange(SEL_BLOCK, dtype=jnp.int32))
        dist_s = dist_s[:, :, None]
        s_s = jnp.einsum('bghqd,bgqnrd->bghqnr', qb, k_sel, preferred_element_type=f32)
        s_s = jnp.where(dist_s >= 0, s_s - slopes[..., None] * dist_s.astype(f32), NEG_INF)
        p_s = jax.nn.softmax(s_s.reshape(B, G, HG, Q_BLOCK, n_sel * SEL_BLOCK), axis=-1).reshape(s_s.shape)
        o_slc = jnp.einsum('bghqnr,bgqnrd->bghqd', p_s.astype(v_sel.dtype), v_sel)
        k_w = lax.dynamic_slice_in_dim(k_win, start, Q_BLOCK + WINDOW, axis=2)
        v_w = lax.dynamic_slice_in_dim(v_win, start, Q_BLOCK + WINDOW, axis=2)
        kpos = start - WINDOW + jnp.arange(Q_BLOCK + WINDOW, dtype=jnp.int32)
        dist_w = t[:, None] - kpos[None, :]
        valid_w = (dist_w >= 0) & (dist_w < WINDOW) & (kpos[None, :] >= 0)
        s_w = jnp.einsum('bghqd,bgkd->bghqk', qb, k_w, preferred_element_type=f32) - slopes * dist_w.astype(f32)
        p_w = jax.nn.softmax(jnp.where(valid_w, s_w, NEG_INF), axis=-1)
        o_win = jnp.einsum('bghqk,bgkd->bghqd', p_w.astype(v_w.dtype), v_w)
        return gb[0][..., None] * o_cmp + gb[1][..., None] * o_slc + gb[2][..., None] * o_win

    o = lax.map(query_block, (q, gates, starts))
    o = jnp.transpose(o, (1, 0, 4, 2, 3, 5)).reshape(B, T, NSA_Q_DIM)
    return o.astype(x.dtype) @ w_out

def setup_inputs(seed: int = 0) -> dict:
    key = jax.random.key(seed)
    ks = jax.random.split(key, 24)
    f32 = jnp.float32

    def dense(k, shape, fan_in):
        return jax.random.normal(k, shape, f32) * fan_in ** -0.5

    def gain(k, shape):
        return 1.0 + 0.02 * jax.random.normal(k, shape, f32)

    x = jax.random.normal(ks[0], (BATCH, SEQ, D_MODEL), f32)
    mixer_norm_g = gain(ks[1], (DEPTH, D_MODEL))
    ffn_norm_g = gain(ks[2], (DEPTH, D_MODEL))
    ffn_w_gate_up = dense(ks[3], (DEPTH, D_MODEL, 2 * FFN_HIDDEN), D_MODEL)
    ffn_w_down = dense(ks[4], (DEPTH, FFN_HIDDEN, D_MODEL), FFN_HIDDEN)
    gdn_w_in = dense(ks[5], (N_A_LAYERS, D_MODEL, GDN_IN_DIM), D_MODEL)
    gdn_conv_w = dense(ks[6], (N_A_LAYERS, GDN_CONV, GDN_CONV_DIM), GDN_CONV)
    gdn_a_log = jnp.log(jax.random.uniform(ks[7], (N_A_LAYERS, GDN_V_HEADS), f32, 1.0, 16.0))
    dt = jnp.exp(jax.random.uniform(ks[8], (N_A_LAYERS, GDN_V_HEADS), f32, math.log(1e-3), math.log(1e-1)))
    gdn_dt_bias = dt + jnp.log(-jnp.expm1(-dt))
    gdn_out_norm_g = gain(ks[9], (N_A_LAYERS, GDN_HEAD_DIM))
    gdn_w_out = dense(ks[10], (N_A_LAYERS, GDN_V_DIM, D_MODEL), GDN_V_DIM)
    kv_norm_g = gain(ks[11], (D_MODEL,))
    kv_w = dense(ks[12], (D_MODEL, NSA_KV_DIM), D_MODEL)
    cmp_pos = 0.02 * jax.random.normal(ks[13], (CMP_BLOCK, NSA_HEAD_DIM), f32)
    cmp_w1_k = dense(ks[14], (CMP_BLOCK * NSA_HEAD_DIM, CMP_HIDDEN), CMP_BLOCK * NSA_HEAD_DIM)
    cmp_w2_k = dense(ks[15], (CMP_HIDDEN, NSA_HEAD_DIM), CMP_HIDDEN)
    cmp_w1_v = dense(ks[16], (CMP_BLOCK * NSA_HEAD_DIM, CMP_HIDDEN), CMP_BLOCK * NSA_HEAD_DIM)
    cmp_w2_v = dense(ks[17], (CMP_HIDDEN, NSA_HEAD_DIM), CMP_HIDDEN)
    nsa_w_in = dense(ks[18], (N_B_LAYERS, D_MODEL, NSA_IN_DIM), D_MODEL)
    nsa_w_out = dense(ks[19], (N_B_LAYERS, NSA_Q_DIM, D_MODEL), NSA_Q_DIM)
    final_norm_g = gain(ks[20], (D_MODEL,))
    return {"x": x, "mixer_norm_g": mixer_norm_g, "ffn_norm_g": ffn_norm_g,
            "ffn_w_gate_up": ffn_w_gate_up, "ffn_w_down": ffn_w_down,
            "gdn_w_in": gdn_w_in, "gdn_conv_w": gdn_conv_w, "gdn_a_log": gdn_a_log,
            "gdn_dt_bias": gdn_dt_bias, "gdn_out_norm_g": gdn_out_norm_g, "gdn_w_out": gdn_w_out,
            "kv_norm_g": kv_norm_g, "kv_w": kv_w, "cmp_pos": cmp_pos,
            "cmp_w1_k": cmp_w1_k, "cmp_w2_k": cmp_w2_k, "cmp_w1_v": cmp_w1_v, "cmp_w2_v": cmp_w2_v,
            "nsa_w_in": nsa_w_in, "nsa_w_out": nsa_w_out, "final_norm_g": final_norm_g}

def reference(x, mixer_norm_g, ffn_norm_g, ffn_w_gate_up, ffn_w_down,
              gdn_w_in, gdn_conv_w, gdn_a_log, gdn_dt_bias, gdn_out_norm_g, gdn_w_out,
              kv_norm_g, kv_w, cmp_pos, cmp_w1_k, cmp_w2_k, cmp_w1_v, cmp_w2_v,
              nsa_w_in, nsa_w_out, final_norm_g):
    h = x
    shared_kv = None
    for layer in range(DEPTH):
        if layer < N_A_LAYERS:
            h = h + gated_deltanet(rms_norm(h, mixer_norm_g[layer]), gdn_w_in[layer], gdn_conv_w[layer],
                                   gdn_a_log[layer], gdn_dt_bias[layer], gdn_out_norm_g[layer], gdn_w_out[layer])
        else:
            j = layer - N_A_LAYERS
            h = h + nsa_attention(rms_norm(h, mixer_norm_g[layer]), shared_kv, nsa_w_in[j], nsa_w_out[j])
        h = h + swiglu_ffn(rms_norm(h, ffn_norm_g[layer]), ffn_w_gate_up[layer], ffn_w_down[layer])
        if layer == N_A_LAYERS - 1:
            shared_kv = nsa_shared_kv(h, kv_norm_g, kv_w, cmp_pos, cmp_w1_k, cmp_w2_k, cmp_w1_v, cmp_w2_v)
    return rms_norm(h, final_norm_g)


_drawn_inputs = setup_inputs


def setup_inputs(seed=0):
    import zlib

    import numpy as np

    out = dict(_drawn_inputs(seed))
    spreads = {}
    factors = {'ffn_norm_g': 3.024,
     'gdn_out_norm_g': 4.061,
     'kv_norm_g': 8.0,
     'cmp_pos': 50.149,
     'final_norm_g': 8.233}
    for name, (base, spread) in spreads.items():
        noise = np.random.default_rng([zlib.crc32(name.encode()), seed]).standard_normal(out[name].shape)
        drawn = base * np.exp(spread * noise) if base else spread * noise
        out[name] = __import__('jax').numpy.asarray(drawn.astype(out[name].dtype))
    for name, factor in factors.items():
        out[name] = (out[name] * factor).astype(out[name].dtype)
    return out
```

```python
import concourse.bass as bass
from concourse import mybir
from contextlib import ExitStack

P = 128
SEQ, DM = 256, 2048
NT = SEQ // P
KT = DM // P
COLS = 512
CHK = 4
CHUNK = CHK * COLS
HEADS = 32
GROUPS = 8
FFN_H = 5632
FBLK = FFN_H // COLS
KVG = 4
CB = 15
CMPB = 32
EPS = 1e-6
RAWS = 4
LEVELS = 6
C_GDN = 16 * GROUPS
C_FFN = 12 * FBLK
C_KV, C_CMP, C_ATT = 24, 8, 32
B_FFN0 = C_GDN
B_KV = B_FFN0 + C_FFN
B_CMP = B_KV + C_KV
B_ATT = B_CMP + C_CMP
B_FFN1 = B_ATT + C_ATT
CHUNKS = B_FFN1 + C_FFN

K_ID, K_TRI, K_ONE, K_LOW, K_STR, K_M1, K_M1T, K_LV = [P * i for i in range(8)]
K_D0 = K_LV + LEVELS * P
K_D1 = K_D0 + P
K_CD = K_D1 + 2 * P
K_CV = K_CD + NT * CB
K_SL = K_CV + NT * CB
K_EPS = K_SL + 16
K_NH = K_EPS + 1
K_END = K_NH + 8
A_CONV, A_GAIN = 0, GROUPS * 32
A_ALOG = A_GAIN + 5 * KT
A_DT = A_ALOG + HEADS
A_ONG = A_DT + HEADS
A_POS = A_ONG + P
A_END = A_POS + CMPB
GW = 36
AW = 28

PREP, SOLVE, ONCE = "prep", "solve", "once"
GDN_STEPS = [
    (7, "gates1", 0, ONCE),
    (0, "y0", 0, SOLVE), (1, "t0", 1, SOLVE), (1, "u0", 0, SOLVE),
    (2, "y1", 0, SOLVE), (3, "t1", 1, SOLVE), (3, "u1", 0, SOLVE),
    (4, "y2", 0, SOLVE), (5, "t2", 1, SOLVE), (5, "u2", 0, SOLVE),
    (6, "y3", 0, SOLVE), (7, "t3", 1, SOLVE), (7, "u3", 0, SOLVE),
    (12, "gates2", 0, ONCE),
    (8, "y4", 0, SOLVE), (9, "t4", 1, SOLVE), (9, "u4", 0, SOLVE), (9, "qk_t", 1, PREP),
    (10, "y5", 0, SOLVE), (10, "conv_qk0", None, PREP), (11, "t5", 1, SOLVE), (11, "u5", 0, SOLVE),
    (12, "nw", 1, SOLVE), (12, "conv_qk1", None, PREP), (13, "ru", 0, SOLVE), (14, "v0", 1, SOLVE),
    (15, "s", 0, SOLVE), (16, "ks", 1, SOLVE), (17, "v1", 0, SOLVE), (17, "v_t", 1, PREP),
    (18, "o", 0, SOLVE), (18, "conv_v0", None, PREP), (19, "osum", None, SOLVE), (20, "conv_v1", None, PREP),
    (20, "oscale", None, SOLVE), (21, "o_t", 1, SOLVE), (22, "silu", None, PREP),
    (24, "ss", 0, PREP), (26, "k_t", 1, PREP), (26, "gb", 0, PREP), (28, "kkqk", 1, PREP), (28, "v_t2", 0, PREP),
    (30, "lt", 1, PREP), (31, "at", 0, PREP)]
GDN_STEPS.sort(key=lambda e: e[0])

PROJ, ATT, OUT = "proj", "att", "out"
ATT_STEPS = [
    (7, "gates", 0, ONCE),
    (0, "sc1a", 0, ATT), (0, "sc0a", 1, ATT), (2, "pt1a", 0, ATT), (2, "pt0a", 1, ATT), (4, "pva", 0, ATT),
    (5, "sc1b", 0, ATT), (5, "sc0b", 1, ATT), (7, "pt1b", 0, ATT), (7, "pt0b", 1, ATT), (9, "pvb", 0, ATT),
    (9, "scc", 1, ATT), (11, "ptc", 0, ATT), (13, "pvc", 1, ATT),
    (15, "o_t", 0, ATT), (15, "q_t", 1, PROJ)]
ATT_STEPS.sort(key=lambda e: e[0])


def steps_at(table, hs, which):
    return [(n, p, w) for h, n, p, w in table if h == hs and w in which]


class Phase:

    def __init__(self, start, lists, lo=0, hi=0, body=()):
        self.start, self.lo, self.hi = dict(start), lo, hi
        self.per = {k: sum(q == k for q, _ in body) for k in start}
        self.base, self.index = {}, {}
        n = dict(start)
        its = sorted([i for i in lists if i < lo]) + (["body"] if hi > lo else []) + sorted(i for i in lists if i >= hi)
        for i in its:
            self.base[i] = dict(n)
            seen = {k: 0 for k in n}
            self.index[i] = {}
            for pair, name in (body if i == "body" else lists[i]):
                self.index[i][name] = (pair, seen[pair])
                seen[pair] += 1
            times = hi - lo if i == "body" else 1
            n = {k: n[k] + times * seen[k] for k in n}
        self.end = n

    def before(self, name, it):
        key = it if isinstance(it, int) and it in self.base else "body"
        pair, at = self.index[key][name]
        value = self.base[key][pair] + at
        return value if key != "body" else (it - self.lo) * self.per[pair] + value

    def after(self, name, it):
        return self.before(name, it) + 1


def gdn_uses(which, proj, outp):
    uses = []
    for hs in range(32):
        j = hs // 2
        if hs % 2 and j in (3, 7, 11) and proj:
            uses.append((f"a{(j // 4) % 2}", f"in{j // 4}"))
        if hs % 2 and j >= 12 and outp:
            uses.append((f"a{(j + 1) % 2}", f"out{j - 12}"))
        uses += [(f"x{p}", n) for n, p, _ in steps_at(GDN_STEPS, hs, which) if p is not None]
    return uses


def ffn_uses(up, down):
    uses = [("a0", "gate"), ("a1", "up")] if up else []
    uses += [(f"a{k % 2}", f"down{k}") for k in range(4)] if down else []
    return uses + ([("x0", "hid_t")] if up else [])


def att_uses(which):
    uses = []
    for hs in range(16):
        if hs == 7 and PROJ in which:
            uses.append(("a0", "q"))
        if hs % 2 and hs >= 9 and OUT in which:
            uses.append((f"a{(hs // 2 + 1) % 2}", f"out{hs // 2 - 4}"))
        uses += [(f"x{p}", n) for n, p, _ in steps_at(ATT_STEPS, hs, which)]
    return uses


NORM_USES = [(f"x{r % 2}", f"norm{r}") for r in range(4)]
KV_USES = []
for _k in range(6):
    KV_USES.append((f"a{_k % 2}", f"kv{_k}"))
    if _k not in (3, 5):
        KV_USES.append((f"x{_k % 2}", f"kv_t{_k}"))
CMP_USES = [("a0", "hid0"), ("a1", "hid1"), ("x0", "hid_t"), ("x1", "w2")]

ZERO = {"a0": 0, "a1": 0, "x0": 0, "x1": 0}
NORM0 = Phase(ZERO, {0: NORM_USES})
GDN = Phase(NORM0.end, {0: gdn_uses((PREP, ONCE), True, False), GROUPS: gdn_uses((SOLVE,), False, True)},
            1, GROUPS, gdn_uses((PREP, SOLVE), True, True))
NORM1 = Phase(GDN.end, {0: NORM_USES})
FFN0 = Phase(NORM1.end, {0: ffn_uses(True, False), FBLK: ffn_uses(False, True)}, 1, FBLK, ffn_uses(True, True))
NORM2 = Phase(FFN0.end, {0: NORM_USES})
KV = Phase(NORM2.end, {0: KV_USES})
CMP = Phase(KV.end, {0: CMP_USES})
NORM3 = Phase(CMP.end, {0: NORM_USES})
ATTN = Phase(NORM3.end, {0: att_uses((PROJ, ONCE)), 1: att_uses((PROJ, ATT)), 4: att_uses((ATT, OUT)),
                         5: att_uses((OUT,))}, 2, KVG, att_uses((PROJ, ATT, OUT)))
NORM4 = Phase(ATTN.end, {0: NORM_USES})
FFN1 = Phase(NORM4.end, {0: ffn_uses(True, False), FBLK: ffn_uses(False, True)}, 1, FBLK, ffn_uses(True, True))


class Chain:

    def __init__(self, eng, semaphore):
        self.eng, self.sem, self.n, self.seen = eng, semaphore, 0, 0

    def link(self, instruction):
        instruction.then_inc(self.sem, 1)
        self.n, self.seen = self.n + 1, self.seen + 1
        self.eng.wait_ge(self.sem, self.n)

    def loop(self, lo, hi, per, body):
        base = self.n
        with self.eng.Fori(lo, hi) as it:
            self.n, self.seen = (it - lo) * per + base, 0
            body(it)
            assert self.seen == per, (self.seen, per)
        self.n = base + (hi - lo) * per


def build(nc, stream, consts, params, tails, w2, gfin, x, out):
    f32, f32r = mybir.dt.float32, mybir.dt.float32r
    ALU, ACT, AX = mybir.AluOpType, mybir.ActivationFunctionType, mybir.AxisListType
    MUL, ADD, SUB = ALU.mult, ALU.add, ALU.subtract
    ds = bass.ds
    D_SC = float(P) ** -0.5
    ONE = dict(start=True, stop=True)
    ctx = ExitStack()

    def sb(name, shape, dt=f32):
        return ctx.enter_context(nc.sbuf_tensor(name, shape, dt))

    def sem(name):
        return ctx.enter_context(nc.semaphore(name))

    def psum(name):
        return ctx.enter_context(nc.psum_tensor(name, [P, NT * COLS], f32))

    with ctx:
        RAW = sb("RAW", [P, RAWS, CHUNK])
        W_HI, W_LO = (sb(n, [P, 2, CHUNK], f32r) for n in ("W_HI", "W_LO"))
        X_HI, X_LO = (sb(n, [P, KT * SEQ], f32r) for n in ("X_HI", "X_LO"))
        A_HI, A_LO = (sb(n, [P, CHK * SEQ], f32r) for n in ("A_HI", "A_LO"))
        H = sb("H", [P, NT, DM])
        K, PRM = sb("K", [P, K_END]), sb("PRM", [P, A_END])
        GA, GP, CW, SM = sb("GA", [P, GROUPS * GW]), sb("GP", [P, GW]), sb("CW", [P, 32]), sb("SM", [P, 24])
        TR, UR, YR, NS0, NS1 = (sb(n, [P, 1024], f32r) for n in ("TR", "UR", "YR", "NS0", "NS1"))
        NS = [NS0, NS1]
        WORK = sb("WORK", [P, 13 * 1024 + 384])
        ACC = [psum(f"ACC{i}") for i in range(2)]
        SIDE = [psum(f"SIDE{i}") for i in range(2)]

        def w(off, n):
            return WORK[:, off:off + n]

        def tiles2(ap):
            return ap.rearrange("p (t n) -> p t n", t=NT)

        def units(ap, n=P):
            return ap.rearrange("p (u n) -> p u n", n=n)

        def each(cols, n=8, width=P):
            return cols.unsqueeze(2).broadcast_to([P, n, width])

        def every(at, n=8):
            return K[:, at:at + P].unsqueeze(1).broadcast_to([P, n, P])

        ident, tri, ones = K[:, K_ID:K_ID + P], K[:, K_TRI:K_TRI + P], K[:, K_ONE:K_ONE + P]
        eps_col, minus_half = K[:, K_EPS:K_EPS + 1], K[:, K_NH:K_NH + 8]
        sumsq_c, rstd_c, rstd_q = SM[:, 0:2], SM[:, 2:4], SM[:, 4:6]
        osum_c, ors_c = SM[:, 8:16], SM[:, 16:24]

        tokraw = w(0, 1024)
        cin = WORK[:, 1024:1024 + 4 * 259].rearrange("p (b n) -> p b n", n=259)
        cq, cv, qkn, vb, E, ES, N, AT, UF, zs = [w(2064 + 1024 * i, 1024) for i in range(10)]
        S, kd = w(2064 + 10240, 512), w(2064 + 10752, 512)
        tailraw = w(7 * 1024, 1024)
        junk = w(8 * 1024, DM)
        sg, hid = w(0, 1024), w(1024, 1024)
        kcT, vc = w(0, 64), WORK[0:CB, 64:576]
        kT = [w(576, 1024), w(1600, 1024)]
        vS = [w(2624, 1024), w(3648, 1024)]
        b0 = 4672
        tkv, kvT = [w(b0, 1024), w(b0 + 1024, 1024)], [w(b0 + 2048, 1024), w(b0 + 3072, 1024)]
        XP, hc, hcT = w(b0 + 4096, 2048), w(b0 + 6144, 512), w(b0 + 6656, 256)
        w2s, tailraw2 = w(b0 + 7168, 512), w(b0 + 7680, KT * 48)
        qtok, qT, sm1, p1T, oacc, tmpo = [w(b0 + 1024 * i, 1024) for i in range(6)]
        sm0, p0T = w(b0 + 6144, 512), w(b0 + 6656, 512)
        pcT = WORK[0:CB, b0 + 7168:b0 + 8192]
        scc, scb, small = w(b0 + 8192, 120), w(b0 + 8320, 120), w(b0 + 8448, 64)
        gsig = w(b0 + 8512, 96)
        hn = tiles2(w(8 * 1024, NT * DM))
        gfs = w(2 * 1024, DM)

        (in_const, tail_in, w2_in, fin_in, pad_zero, hi_ready, lo_ready, w_used, x_hi, sumsq, rstd, tail_hi, tail_lo,
         gate_abs, gate_exp, gate_ea, gate_ln, gate_g, gate_cum, gate_fac, conv_done, silu_done, sq_done, rb_done,
         qkn_done, gp_ready, gbc_done, dif_done, exp_done, decay_ready, tu_ready, ns_ready, osq_done, osum_done,
         ors_done, o_scaled, zg_ready, act_hi, xp_done, xp_hi, xp_lo, mx_done, p_exp, sc_max, sc_exp, pc_ready,
         att_done, y_done, out_done, dve_chain, pool_chain) = (sem(n) for n in (
             "in_const tail_in w2_in fin_in pad_zero hi_ready lo_ready w_used x_hi sumsq rstd tail_hi tail_lo "
             "gate_abs gate_exp gate_ea gate_ln gate_g gate_cum gate_fac conv_done silu_done sq_done rb_done "
             "qkn_done gp_ready gbc_done dif_done exp_done decay_ready tu_ready ns_ready osq_done osum_done "
             "ors_done o_scaled zg_ready act_hi xp_done xp_hi xp_lo mx_done p_exp sc_max sc_exp pc_ready "
             "att_done y_done out_done dve_chain pool_chain").split())
        raw_full = [sem(f"raw_full{i}") for i in range(RAWS)]
        acc_out = [sem(f"acc_out{i}") for i in range(2)]
        side_full = [sem(f"side_full{i}") for i in range(2)]
        side_out = [sem(f"side_out{i}") for i in range(2)]

        def wait_past(eng, semaphore, n):
            if not (isinstance(n, int) and n == 0):
                eng.wait_ge(semaphore, n)

        def gdn_c(it):
            return {0: 0, GROUPS: 16 * (GROUPS - 1)}[it] if isinstance(it, int) else it * 16 - 4

        def ffn_c(base, it):
            return {0: base, FBLK: base + 12 * (FBLK - 1)}[it] if isinstance(it, int) else it * 12 + (base - 4)

        def att_c(it):
            return B_ATT + {0: 0, 1: 4, 4: 20, 5: 24}[it] if isinstance(it, int) else it * 8 + (B_ATT - 8)

        def gdn_which(it):
            return {0: (PREP, ONCE), GROUPS: (SOLVE,)}.get(it, (PREP, SOLVE)) if isinstance(it, int) else (PREP, SOLVE)

        def att_which(it):
            every_ = (PROJ, ATT, OUT)
            return {0: (PROJ, ONCE), 1: (PROJ, ATT), 4: (ATT, OUT), 5: (OUT,)}[it] if isinstance(it, int) else every_

        def products(pe, c, k, acc, hi, lo, first, last, half, base=0):
            if half == 0:
                pe.wait_ge(lo_ready, c + (k + 1))
            for q in (2 * half, 2 * half + 1):
                for t in range(NT):
                    dst = ACC[acc][:, t * COLS:(t + 1) * COLS]
                    at = (base + q) * SEQ + t * P
                    wh, wl = (b[:, k % 2, q * COLS:(q + 1) * COLS] for b in (W_HI, W_LO))
                    nc.tensor.matmul(dst, hi[:, at:at + P], wh, start=first and q == 0, stop=False)
                    nc.tensor.matmul(dst, hi[:, at:at + P], wl, start=False, stop=False)
                    m = nc.tensor.matmul(dst, lo[:, at:at + P], wh, start=False, stop=last and q == 3)
            if half:
                m.then_inc(w_used, 1)

        def turn(pairs, p):
            for to, src in pairs:
                m = nc.tensor.transpose(SIDE[p][:, to:to + P], src, ident)
            m.then_inc(side_full[p], 1)

        def by_block(buf):
            return [((b * NT + t) * P, buf[:, t * COLS + b * P:t * COLS + (b + 1) * P])
                    for b in range(4) for t in range(NT)]

        def by_unit(buf):
            return [((hl * NT + t) * P, buf[:, (t * 4 + hl) * P:(t * 4 + hl + 1) * P])
                    for t in range(NT) for hl in range(4)]

        def norm_tensor(pe, norm, r, ready):
            wait_past(pe, side_out[r % 2], norm.before(f"norm{r}", 0))
            if ready:
                pe.wait_ge(acc_out[ready[0]], ready[1])
            turn([((q * NT + t) * P, H[:, t, (4 * r + q) * P:(4 * r + q + 1) * P]) for q in range(4)
                  for t in range(NT)], r % 2)

        def tail_tensor(pe, nth, n, width):
            wait_past(pe, side_out[0], n)
            pe.wait_ge(tail_lo, nth + 1)
            for t in range(NT):
                dst = SIDE[0][:, t * COLS:t * COLS + width]
                for kt in range(KT):
                    at = kt * SEQ + t * P
                    wh, wl = (b[:, kt * width:(kt + 1) * width] for b in (A_HI, A_LO))
                    nc.tensor.matmul(dst, X_HI[:, at:at + P], wh, start=kt == 0, stop=False)
                    nc.tensor.matmul(dst, X_HI[:, at:at + P], wl, start=False, stop=False)
                    m = nc.tensor.matmul(dst, X_LO[:, at:at + P], wh, start=False, stop=kt == KT - 1)
            m.then_inc(side_full[0], 1)

        def unit_products(p, lhs, rhs, n=8, at=0):
            for u in range(n):
                m = nc.tensor.matmul(SIDE[p][:, u * P:(u + 1) * P], lhs[:, at + u * P:at + (u + 1) * P],
                                     rhs[:, u * P:(u + 1) * P], **ONE)
            m.then_inc(side_full[p], 1)

        def gdn_step_tensor(pe, name, p, g, it):
            if p is None:
                return
            wait_past(pe, side_out[p], GDN.before(name, it))
            dst = SIDE[p]
            kind, lv = name[0], int(name[1:]) if name[1:].isdigit() else None
            if name == "gates1":
                tail_tensor(pe, 0, 0, 64)
            elif name == "gates2":
                pe.wait_ge(gate_g, 1)
                for t in range(NT):
                    nc.tensor.matmul(dst[:, 32 * t:32 * t + 32], tri, gg[:, t, :], **ONE)
                nc.tensor.matmul(dst[:, 64:96], ones, gg[:, 0, :], **ONE).then_inc(side_full[0], 1)
            elif name == "qk_t":
                pe.wait_ge(acc_out[0], GDN.after("in0", it))
                turn(by_block(tokraw), p)
            elif name == "v_t":
                pe.wait_ge(acc_out[1], GDN.after("in1", it))
                turn(by_block(tokraw), p)
            elif name == "ss":
                pe.wait_ge(sq_done, g + 1)
                for i in range(2):
                    m = nc.tensor.matmul(dst[:, i * 512:(i + 1) * 512], ones, ES[:, i * 512:(i + 1) * 512], **ONE)
                m.then_inc(side_full[p], 1)
            elif name == "k_t":
                pe.wait_ge(qkn_done, g + 1)
                turn([(hq * P, qkn[:, 512 + hq * SEQ:512 + hq * SEQ + P]) for hq in range(2)], p)
            elif name == "gb":
                pe.wait_ge(gbc_done, g + 1)
                for u in range(8):
                    m = nc.tensor.matmul(dst[:, u * P:(u + 1) * P], E[:, u * P:(u + 1) * P], tri, **ONE)
                m.then_inc(side_full[p], 1)
            elif name == "kkqk":
                pe.wait_ge(qkn_done, g + 1)
                for of in range(2):
                    for t in range(NT):
                        for hq in range(2):
                            a = hq * SEQ + t * P
                            kk = qkn[:, 512 + a:512 + a + P]
                            to = of * 512 + (t * 2 + hq) * P
                            m = nc.tensor.matmul(dst[:, to:to + P], qkn[:, a:a + P] if of else kk, kk, **ONE)
                m.then_inc(side_full[p], 1)
            elif name == "v_t2":
                pe.wait_ge(silu_done, 2 * g + 2)
                turn([((t * 4 + hl) * P, cv[:, hl * SEQ + t * P:hl * SEQ + (t + 1) * P])
                      for t in range(NT) for hl in range(4)], p)
            elif name in ("lt", "at"):
                pe.wait_ge(side_out[1], GDN.after("kkqk", it))
                src = ES if name == "lt" else E
                turn([(u * P, src[:, u * P:(u + 1) * P]) for u in range(8)], p)
            elif kind == "y":
                pe.wait_ge(ns_ready, g * LEVELS + lv + 1)
                if lv == 0:
                    pe.wait_ge(tu_ready, g + 1)
                else:
                    pe.wait_ge(side_out[1], GDN.after(f"t{lv - 1}", it))
                unit_products(p, NS[lv % 2], TR)
            elif kind == "t":
                pe.wait_ge(side_out[0], GDN.after(f"y{lv}", it))
                unit_products(p, UR, YR)
            elif kind == "u":
                unit_products(p, YR, UR)
            elif name == "nw":
                pe.wait_ge(side_out[1], GDN.after("t5", it))
                unit_products(p, N, TR[:, :].bitcast(f32))
            elif name == "ru":
                pe.wait_ge(side_out[1], GDN.after("nw", it))
                unit_products(p, YR, UR)
            elif name == "v0":
                pe.wait_ge(side_out[0], GDN.after("ru", it))
                unit_products(p, UF, vb, 4)
            elif name == "s":
                pe.wait_ge(side_out[1], GDN.after("v0", it))
                unit_products(p, kd, E, 4)
            elif name == "ks":
                pe.wait_ge(side_out[0], GDN.after("s", it))
                for of in range(2):
                    for hq in range(2):
                        a = (0 if of else 512) + hq * SEQ + P
                        m = nc.tensor.matmul(dst[:, of * 512 + hq * SEQ:of * 512 + (hq + 1) * SEQ], qkn[:, a:a + P],
                                             S[:, hq * SEQ:(hq + 1) * SEQ], **ONE)
                m.then_inc(side_full[p], 1)
            elif name == "v1":
                pe.wait_ge(side_out[1], GDN.after("ks", it))
                unit_products(p, UF, vb[:, 512:1024], 4, 512)
            elif name == "o":
                pe.wait_ge(side_out[0], GDN.after("v1", it))
                unit_products(p, AT, E)
            elif name == "o_t":
                pe.wait_ge(o_scaled, g + 1)
                turn(by_unit(ES), p)

        def gdn_tensor(pe, it):
            c, which = gdn_c(it), gdn_which(it)
            for hs in range(32):
                j, half = hs // 2, hs % 2
                if j < 12 and PREP in which:
                    acc, k = (j // 4) % 2, j % 4
                    if half == 0 and k == 0:
                        wait_past(pe, acc_out[acc], GDN.before(f"in{j // 4}", it))
                    if half == 0 and ONCE in which and j < 4:
                        pe.wait_ge(side_out[j % 2], NORM0.after(f"norm{j}", 0))
                    products(pe, c, j, acc, X_HI, X_LO, k == 0, k == 3, half, 4 * k)
                if j >= 12 and SOLVE in which:
                    acc = (j + 1) % 2
                    if half == 0:
                        pe.wait_ge(acc_out[acc], GDN.before(f"out{j - 12}", it))
                        if j == 12:
                            pe.wait_ge(side_out[1], GDN.after("o_t", it))
                    products(pe, c, j, acc, A_HI, A_LO, True, True, half)
                    if half and j > 12 and PREP not in which:
                        norm_tensor(pe, NORM1, j - 13, ((j - 13 + 1) % 2, GDN.after(f"out{j - 13}", it)))
                for name, p, w_ in steps_at(GDN_STEPS, hs, which):
                    gdn_step_tensor(pe, name, p, it - 1 if w_ == SOLVE else it, it)
            if PREP not in which:
                norm_tensor(pe, NORM1, 3, (0, GDN.after("out3", it)))

        def ffn_tensor(pe, ph, base, norm, it, nxt):
            c = ffn_c(base, it)
            first = isinstance(it, int) and it == 0
            final_ = isinstance(it, int) and it == FBLK
            for k in range(12):
                if k < 8 and not final_:
                    if k % 4 == 0:
                        pe.wait_ge(acc_out[k // 4], ph.before("up" if k else "gate", it))
                    if first and k < 4:
                        pe.wait_ge(side_out[k % 2], norm.after(f"norm{k}", 0))
                    for half in range(2):
                        products(pe, c, k, k // 4, X_HI, X_LO, k % 4 == 0, k % 4 == 3, half, 4 * (k % 4))
                if k >= 8 and not first:
                    pe.wait_ge(acc_out[k % 2], ph.before(f"down{k - 8}", it))
                    if k == 8:
                        pe.wait_ge(side_out[0], ph.before("hid_t", it) if not final_ else ph.end["x0"])
                    for half in range(2):
                        products(pe, c, k, k % 2, A_HI, A_LO, True, True, half)
                    if final_ and nxt and k > 8:
                        norm_tensor(pe, nxt, k - 9, ((k - 9) % 2, ph.after(f"down{k - 9}", it)))
            if not final_:
                pe.wait_ge(side_out[0], ph.before("hid_t", it))
                pe.wait_ge(acc_out[1], ph.after("up", it))
                turn(by_block(hid), 0)
            elif nxt:
                norm_tensor(pe, nxt, 3, (1, ph.after("down3", it)))

        def kv_tensor(pe):
            for s in range(6):
                acc = s % 2
                pe.wait_ge(acc_out[acc], KV.before(f"kv{s}", 0))
                for k in range(4):
                    if s == 0:
                        pe.wait_ge(side_out[k % 2], NORM2.after(f"norm{k}", 0))
                    for half in range(2):
                        products(pe, B_KV, 4 * s + k, acc, X_HI, X_LO, k == 0, k == 3, half, 4 * k)
                if s not in (3, 5):
                    pe.wait_ge(side_out[acc], KV.before(f"kv_t{s}", 0))
                    pe.wait_ge(acc_out[acc], KV.after(f"kv{s}", 0))
                    turn(by_block(tkv[acc]), acc)

        def compress_tensor(pe):
            for kv in range(2):
                pe.wait_ge(xp_lo, kv + 1)
                pe.wait_ge(acc_out[kv], CMP.before(f"hid{kv}", 0))
                for k in range(4):
                    c = 4 * kv + k
                    pe.wait_ge(lo_ready, B_CMP + c + 1)
                    for q in range(8):
                        at = kv * 2048 + (8 * k + q) * 60
                        wh, wl = (b[:, c % 2, q * 256:(q + 1) * 256] for b in (W_HI, W_LO))
                        d = ACC[kv][:, 0:256]
                        nc.tensor.matmul(d, X_HI[:, at:at + P], wh, start=k == 0 and q == 0, stop=False)
                        nc.tensor.matmul(d, X_HI[:, at:at + P], wl, start=False, stop=False)
                        m = nc.tensor.matmul(d, X_LO[:, at:at + P], wh, start=False, stop=k == 3 and q == 7)
                    m.then_inc(w_used, 1)
            for kv in range(2):
                pe.wait_ge(acc_out[kv], CMP.after(f"hid{kv}", 0))
            pe.wait_ge(side_out[0], CMP.before("hid_t", 0))
            for i in range(4):
                m = nc.tensor.transpose(SIDE[0][:, i * 64:i * 64 + 60], hc[0:60, i * P:(i + 1) * P],
                                        K[0:60, K_ID:K_ID + 60])
            m.then_inc(side_full[0], 1)
            pe.wait_ge(side_out[1], CMP.before("w2", 0))
            pe.wait_ge(side_out[0], CMP.after("hid_t", 0))
            pe.wait_ge(w2_in, 16)
            for kt in range(2):
                nc.tensor.matmul(SIDE[1][:, 0:60], w2s[:, kt * P:(kt + 1) * P], hcT[:, kt * 64:kt * 64 + 60],
                                 start=kt == 0, stop=kt == 1)
            for gq in range(KVG):
                for kt in range(2):
                    at = (2 + kt) * 64 + gq * CB
                    m = nc.tensor.matmul(SIDE[1][0:CB, COLS + gq * P:COLS + (gq + 1) * P], hcT[:, at:at + CB],
                                         w2s[:, 256 + kt * P:256 + (kt + 1) * P], start=kt == 0, stop=kt == 1)
            m.then_inc(side_full[1], 1)

        def att_step_tensor(pe, name, p, g, it):
            wait_past(pe, side_out[p], ATTN.before(name, it))
            dst = SIDE[p]
            b = "ab".find(name[-1])
            if name == "gates":
                tail_tensor(pe, 1, ATTN.before(name, it), 48)
            elif name[:3] == "sc1":
                if b == 0:
                    pe.wait_ge(side_out[1], ATTN.before("sc0a", it))
                for hl in range(4):
                    m = nc.tensor.matmul(dst[:, hl * SEQ:(hl + 1) * SEQ], qT[:, hl * SEQ + P:(hl + 1) * SEQ],
                                         kT[b][:, ds(g * SEQ, SEQ)], **ONE)
                m.then_inc(side_full[p], 1)
            elif name[:3] == "sc0":
                for hl in range(4):
                    m = nc.tensor.matmul(dst[:, hl * P:(hl + 1) * P], qT[:, hl * SEQ:hl * SEQ + P],
                                         kT[b][:, ds(g * SEQ, P)], **ONE)
                m.then_inc(side_full[p], 1)
            elif name[:3] == "pt1":
                pe.wait_ge(p_exp, g * 4 + 2 * b + 1)
                turn([(i * P, sm1[:, i * P:(i + 1) * P]) for i in range(8)], p)
            elif name[:3] == "pt0":
                pe.wait_ge(p_exp, g * 4 + 2 * b + 2)
                turn([(i * P, sm0[:, i * P:(i + 1) * P]) for i in range(4)], p)
            elif name[:2] == "pv" and b >= 0:
                pe.wait_ge(side_out[0], ATTN.after(f"pt1{name[-1]}", it))
                pe.wait_ge(side_out[1], ATTN.after(f"pt0{name[-1]}", it))
                for hl in range(4):
                    nc.tensor.matmul(dst[:, hl * P:(hl + 1) * P], p0T[:, hl * P:(hl + 1) * P],
                                     vS[b][:, ds(g * P, P)], **ONE)
                    for kt in range(2):
                        m = nc.tensor.matmul(dst[:, (4 + hl) * P:(5 + hl) * P],
                                             p1T[:, (hl * 2 + kt) * P:(hl * 2 + kt + 1) * P],
                                             vS[b][:, ds(g * P + kt * COLS, P)], start=kt == 0, stop=kt == 1)
                m.then_inc(side_full[p], 1)
            elif name == "scc":
                for u in range(8):
                    at = (u % 4) * SEQ + (u // 4) * P
                    m = nc.tensor.matmul(dst[:, u * CB:(u + 1) * CB], qT[:, at:at + P], kcT[:, ds(g * CB, CB)], **ONE)
                m.then_inc(side_full[p], 1)
            elif name == "ptc":
                pe.wait_ge(pc_ready, g + 1)
                for u in range(8):
                    m = nc.tensor.transpose(dst[0:CB, u * P:(u + 1) * P], scc[:, u * CB:(u + 1) * CB], ident)
                m.then_inc(side_full[p], 1)
            elif name == "pvc":
                pe.wait_ge(side_out[0], ATTN.after("ptc", it))
                for u in range(8):
                    m = nc.tensor.matmul(dst[:, u * P:(u + 1) * P], pcT[:, u * P:(u + 1) * P],
                                         vc[:, ds(g * P, P)], **ONE)
                m.then_inc(side_full[p], 1)
            elif name == "o_t":
                pe.wait_ge(att_done, g + 1)
                turn(by_unit(oacc), p)
            elif name == "q_t":
                pe.wait_ge(acc_out[0], ATTN.after("q", it))
                turn(by_block(qtok), p)

        def att_tensor(pe, it):
            c, which = att_c(it), att_which(it)
            for hs in range(16):
                j, half = hs // 2, hs % 2
                if j < 4 and PROJ in which:
                    if hs == 0:
                        pe.wait_ge(acc_out[0], ATTN.before("q", it))
                    if half == 0 and ONCE in which:
                        pe.wait_ge(side_out[j % 2], NORM3.after(f"norm{j}", 0))
                    products(pe, c, j, 0, X_HI, X_LO, j == 0, j == 3, half, 4 * j)
                if j >= 4 and OUT in which:
                    acc = (j + 1) % 2
                    if half == 0:
                        pe.wait_ge(acc_out[acc], ATTN.before(f"out{j - 4}", it))
                        if j == 4:
                            pe.wait_ge(side_out[0], ATTN.before("sc1a", it) if ATT in which else ATTN.end["x0"])
                    products(pe, c, j, acc, A_HI, A_LO, True, True, half)
                    if half and j > 4 and ATT not in which:
                        norm_tensor(pe, NORM4, j - 5, (j % 2, ATTN.after(f"out{j - 5}", it)))
                for name, p, w_ in steps_at(ATT_STEPS, hs, which):
                    att_step_tensor(pe, name, p, it - 1 if w_ == ATT else it, it)
            if ATT not in which and OUT in which:
                norm_tensor(pe, NORM4, 3, (0, ATTN.after("out3", it)))

        def split_hi(act, c, k):
            if isinstance(c, int) and c + k >= CHUNKS:
                return
            act.wait_ge(raw_full[k % RAWS], c * 4 + 16 * (k // RAWS + 1))
            if not (isinstance(c, int) and c + k < 2):
                act.wait_ge(w_used, c + (k - 1))
            nc.scalar.activation(W_HI[:, k % 2, :], RAW[:, k % RAWS, :], ACT.Copy).then_inc(hi_ready, 1)

        def take_out(act, p, n, dst, src=None, func=ACT.Copy, **more):
            act.wait_ge(side_full[p], n)
            nc.scalar.activation(dst, SIDE[p][:, :] if src is None else src, func, **more).then_inc(side_out[p], 1)

        def stripe_out(acc, dst, scale, func=ACT.Copy):
            for t in range(NT):
                i = nc.scalar.activation(dst[:, t * COLS:(t + 1) * COLS], ACC[acc][:, t * COLS:(t + 1) * COLS], func,
                                         scale=scale[:, t:t + 1])
            i.then_inc(acc_out[acc], 1)

        def norm_scalar(act, norm, nth, r, gain):
            act.wait_ge(side_full[r % 2], norm.after(f"norm{r}", 0))
            for q in range(4):
                kt = 4 * r + q
                i = nc.scalar.activation(X_HI[:, kt * SEQ:(kt + 1) * SEQ], SIDE[r % 2][:, q * SEQ:(q + 1) * SEQ],
                                         ACT.Copy, scale=PRM[:, A_GAIN + gain * KT + kt:A_GAIN + gain * KT + kt + 1])
            i.then_inc(x_hi, 1)

        def squares(act, nth, ready, to):
            for p in range(2):
                if ready:
                    act.wait_ge(acc_out[p], ready[f"a{p}"])
            for t in range(NT):
                if t:
                    act.wait_ge(sumsq, 2 * nth + 1)
                nc.scalar.activation(to[t], H[:, t, :], ACT.Square, accum_out=sumsq_c[:, t:t + 1]).then_inc(sumsq, 1)

        def act_in_scalar(act, p, n, used):
            act.wait_ge(w_used, used)
            act.wait_ge(side_full[p], n)
            nc.scalar.activation(A_HI[:, :], SIDE[p][:, :], ACT.Copy).then_inc(act_hi, 1)

        def tail_scalar(act, nth, raw):
            act.wait_ge(tail_in, 16 * nth + 16)
            nc.scalar.activation(A_HI[:, 0:raw.shape[1]], raw, ACT.Copy).then_inc(tail_hi, 1)

        def gdn_step_scalar(act, name, p, g, it, used):
            n = GDN.after(name, it) if p is not None else None
            kind = name[0] if name[1:].isdigit() else name
            if name == "gates1":
                act.wait_ge(gate_abs, 1)
                nc.scalar.activation(bet, bav[:, :, 0:32], ACT.Exp, scale=-1.0).then_inc(gate_exp, 1)
                nc.scalar.activation(eal, PRM[:, A_ALOG:A_ALOG + HEADS], ACT.Exp).then_inc(gate_ea, 1)
                nc.scalar.activation(spl, spl, ACT.Exp, scale=-1.0).then_inc(gate_exp, 1)
                act.wait_ge(gate_exp, 2)
                nc.scalar.activation(spl, spl, ACT.Ln, bias=1.0).then_inc(gate_ln, 1)
            elif name == "gates2":
                act.wait_ge(gate_cum, 1)
                nc.scalar.activation(egc, gcl[:, 32:64], ACT.Exp).then_inc(gate_fac, 1)
                nc.scalar.activation(kdx, kdx, ACT.Exp).then_inc(gate_fac, 1)
            elif name in ("qk_t", "v_t"):
                wait_past(act, conv_done, g * 4 + (2 if name == "v_t" else 0))
                take_out(act, p, n, cin[:, :, 3:3 + SEQ], SIDE[p][:, :].rearrange("p (b n) -> p b n", n=SEQ))
            elif name == "silu":
                act.wait_ge(conv_done, g * 4 + 4)
                nc.scalar.activation(cq, cq, ACT.Silu).then_inc(silu_done, 1)
                nc.scalar.activation(cv, cv, ACT.Silu).then_inc(silu_done, 1)
                act.wait_ge(silu_done, g * 2 + 1)
                if not isinstance(it, int):
                    act.wait_ge(side_full[1], GDN.after("o_t", it))
                nc.scalar.activation(ES, cq, ACT.Square).then_inc(sq_done, 1)
            elif name == "ss":
                take_out(act, p, n, ES, func=ACT.Ln, bias=eps_col)
                act.wait_ge(side_out[p], n)
                nc.scalar.activation(ES, ES, ACT.Exp, scale=-0.5).then_inc(rb_done, 1)
            elif name == "gb":
                act.wait_ge(dif_done, g + 1)
                nc.scalar.activation(E, E, ACT.Exp).then_inc(exp_done, 1)
            elif name == "lt":
                take_out(act, p, n, N)
            elif name == "at":
                take_out(act, p, n, AT)
            elif kind == "y":
                take_out(act, p, n, YR[:, :])
            elif name == "v0":
                take_out(act, p, n, E[:, 0:512], SIDE[p][:, 0:512])
            elif name == "s":
                take_out(act, p, n, S, SIDE[p][:, 0:512])
            elif name == "v1":
                take_out(act, p, n, E[:, 512:1024], SIDE[p][:, 0:512])
            elif name == "osum":
                act.wait_ge(side_out[0], GDN.after("o", it))
                nc.scalar.activation(N, ES, ACT.Square).then_inc(osq_done, 1)
            elif name == "o_t":
                act_in_scalar(act, p, n, used)

        def gdn_scalar(act, it):
            c, which = gdn_c(it), gdn_which(it)
            for hs in range(32):
                j = hs // 2
                on = (PREP if j < 12 else SOLVE) in which
                if hs % 2 and on:
                    split_hi(act, c, j + 2)
                    if j % 4 == 3 and j < 12:
                        act.wait_ge(w_used, c + (j + 1))
                        if ONCE in which:
                            act.wait_ge(rstd, 1)
                        if j == 11:
                            wait_past(act, o_scaled, it)
                            stripe_out(0, zs, rstd_c, ACT.Silu)
                        else:
                            stripe_out(j // 4, tokraw, rstd_c)
                    if j > 12 and PREP not in which:
                        norm_scalar(act, NORM1, 1, j - 13, 1)
                for name, p, w_ in steps_at(GDN_STEPS, hs, which):
                    gdn_step_scalar(act, name, p, it - 1 if w_ == SOLVE else it, it, c if PREP in which else c + 12)
            if PREP not in which:
                norm_scalar(act, NORM1, 1, 3, 1)
                squares(act, 1, GDN.end, [junk, junk])

        def ffn_scalar(act, ph, base, it, nrm, nxt):
            c = ffn_c(base, it)
            first, final_ = (isinstance(it, int) and it == n for n in (0, FBLK))
            for k in range(12):
                if (k < 8 and final_) or (k >= 8 and first):
                    continue
                split_hi(act, c, k + 2)
                if k == 3:
                    act.wait_ge(w_used, c + 4)
                    act.wait_ge(acc_out[1], ph.before("up", it))
                    if first:
                        act.wait_ge(rstd, nrm)
                    stripe_out(0, sg, rstd_c, ACT.Silu)
                if k > 8 and final_ and nxt:
                    norm_scalar(act, nxt[0], nxt[1], k - 9, nxt[2])
            if not final_:
                act_in_scalar(act, 0, ph.after("hid_t", it), c + (8 if first else 12))
            elif nxt:
                norm_scalar(act, nxt[0], nxt[1], 3, nxt[2])
                squares(act, 2, ph.end, [junk, junk])

        def kv_scalar(act):
            act.wait_ge(rstd, 3)
            for s in range(6):
                acc = s % 2
                for k in range(4):
                    split_hi(act, B_KV, 4 * s + k + 2)
                act.wait_ge(w_used, B_KV + 4 * s + 4)
                stripe_out(acc, vS[(s - 3) // 2] if s in (3, 5) else tkv[acc], rstd_c)
                if s not in (3, 5):
                    take_out(act, acc, KV.after(f"kv_t{s}", 0), {0: kvT[0], 1: kvT[1], 2: kT[0], 4: kT[1]}[s])

        def compress_scalar(act):
            for kv in range(2):
                act.wait_ge(xp_done, kv + 1)
                nc.scalar.activation(X_HI[:, kv * 2048:kv * 2048 + 1920], XP[:, 0:1920], ACT.Copy).then_inc(xp_hi, 1)
            for kv in range(2):
                for k in range(4):
                    split_hi(act, B_CMP, 4 * kv + k + 2)
                act.wait_ge(w_used, B_CMP + 4 * kv + 4)
                nc.scalar.activation(hc[0:60, kv * 256:(kv + 1) * 256], ACC[kv][0:60, 0:256], ACT.Silu)\
                  .then_inc(acc_out[kv], 1)
            def rows(ap):
                return ap.rearrange("p (i n) -> p i n", n=64)[:, :, 0:60]
            take_out(act, 0, CMP.after("hid_t", 0), rows(hcT), rows(SIDE[0][:, 0:256]))
            act.wait_ge(side_full[1], CMP.after("w2", 0))
            nc.scalar.activation(kcT[:, 0:60], SIDE[1][:, 0:60], ACT.Copy)
            nc.scalar.activation(vc, SIDE[1][0:CB, COLS:2 * COLS], ACT.Copy).then_inc(side_out[1], 1)

        def att_step_scalar(act, name, p, g, it, used):
            n = ATTN.after(name, it)
            b = "ab".find(name[-1])
            if name == "gates":
                act.wait_ge(side_full[0], n)
                for t in range(NT):
                    i = nc.scalar.activation(gsig[:, t * 48:(t + 1) * 48], SIDE[0][:, t * COLS:t * COLS + 48], ACT.Exp,
                                             scale=SM[:, 6 + t:7 + t])
                i.then_inc(side_out[0], 1)
            elif name[:2] == "sc" and b >= 0:
                t = int(name[2])
                sm, wd = (sm1, SEQ) if t else (sm0, P)
                act.wait_ge(mx_done, g * 4 + (2 * b + 2 - t))
                for hl in range(4):
                    part = sm[:, hl * wd:(hl + 1) * wd]
                    at = b * 8 + t * 4 + hl
                    i = nc.scalar.activation(part, part, ACT.Exp, bias=mxs[:, t * 4 + hl:t * 4 + hl + 1],
                                             accum_out=sums[:, at:at + 1])
                i.then_inc(p_exp, 1)
            elif name[:3] == "pt1":
                take_out(act, p, n, p1T)
            elif name[:3] == "pt0":
                take_out(act, p, n, p0T, SIDE[1][:, 0:512])
            elif name == "scc":
                act.wait_ge(sc_max, g + 1)
                nc.scalar.activation(scc, scc, ACT.Exp).then_inc(sc_exp, 1)
            elif name == "ptc":
                take_out(act, p, n, pcT, SIDE[0][0:CB, :])
            elif name == "o_t":
                act_in_scalar(act, p, n, used)
            elif name == "q_t":
                take_out(act, p, n, qT)

        def att_scalar(act, it):
            c, which = att_c(it), att_which(it)
            for hs in range(16):
                j = hs // 2
                if hs % 2 and (PROJ if j < 4 else OUT) in which:
                    split_hi(act, c, j + 2)
                    if j == 3:
                        act.wait_ge(w_used, c + 4)
                        stripe_out(0, qtok, rstd_q)
                    if j > 4 and ATT not in which:
                        norm_scalar(act, NORM4, 4, j - 5, 4)
                for name, p, w_ in steps_at(ATT_STEPS, hs, which):
                    att_step_scalar(act, name, p, it - 1 if w_ == ATT else it, it, c + (8 if OUT in which else 4))
            if ATT not in which and OUT in which:
                norm_scalar(act, NORM4, 4, 3, 4)
                squares(act, 3, ATTN.end, [junk, junk])

        def split_lo(dve, c, k):
            if isinstance(c, int) and c + k >= CHUNKS:
                return
            dve.wait_ge(hi_ready, c + (k + 1))
            nc.vector.tensor_tensor(W_LO[:, k % 2, :], RAW[:, k % RAWS, :], W_HI[:, k % 2, :].bitcast(f32),
                                    SUB).then_inc(lo_ready, 1)

        def norm_vector(dve, norm, nth, r, gain):
            dve.wait_ge(x_hi, 4 * nth + r + 1)
            for q in range(4):
                kt = 4 * r + q
                at = slice(kt * SEQ, (kt + 1) * SEQ)
                i = nc.vector.scalar_tensor_tensor(X_LO[:, at], SIDE[r % 2][:, q * SEQ:(q + 1) * SEQ],
                                                   PRM[:, A_GAIN + gain * KT + kt:A_GAIN + gain * KT + kt + 1],
                                                   X_HI[:, at].bitcast(f32), MUL, SUB)
            i.then_inc(side_out[r % 2], 1)

        def add_to_h(dve, c, k, acc, stripe):
            dve.wait_ge(w_used, c + (k + 1))
            dst = H[:, :, stripe * COLS:(stripe + 1) * COLS]
            nc.vector.tensor_tensor(dst, dst, tiles2(ACC[acc][:, :]), ADD).then_inc(acc_out[acc], 1)

        def act_in_vector(dve, p, nth):
            dve.wait_ge(act_hi, nth)
            nc.vector.tensor_tensor(A_LO[:, :], SIDE[p][:, :], A_HI[:, :].bitcast(f32), SUB).then_inc(side_out[p], 1)

        def tail_vector(dve, nth, raw):
            dve.wait_ge(tail_hi, nth + 1)
            n = raw.shape[1]
            nc.vector.tensor_tensor(A_LO[:, 0:n], raw, A_HI[:, 0:n].bitcast(f32), SUB).then_inc(tail_lo, 1)

        ba = w(12 * 1024, 512)
        bav, bet, spl, gg = (tiles2(ba[:, a:b]) for a, b in ((0, 128), (128, 192), (192, 256), (256, 320)))
        gcl, eal, kdx, egc = ba[:, 320:416], ba[:, 416:448], ba[:, 448:480], ba[:, 480:512]
        GAg = GA[:, :].rearrange("p (g c) -> p g c", c=GW)

        def heads(ap):
            return ap.rearrange("p (g h) -> p g h", h=4)

        def conv(link, dst, nth, blocks):
            for tap in range(4):
                for b in blocks:
                    wc = CW[:, 16 * nth + 4 * b + tap:16 * nth + 4 * b + tap + 1]
                    d, src = dst[:, b * SEQ:(b + 1) * SEQ], cin[:, b, tap:tap + SEQ]
                    if tap == 0:
                        i = nc.vector.tensor_scalar(d, src, wc, None, MUL)
                    else:
                        i = nc.vector.scalar_tensor_tensor(d, src, wc, d, MUL, ADD)
                if tap < 3:
                    link(i)
            i.then_inc(conv_done, 1)

        def gates1_vector(dve, link, n):
            dve.wait_ge(side_full[0], n)
            dve.wait_ge(rstd, 1)
            for t in range(NT):
                i = nc.vector.tensor_scalar(bav[:, t, 0:64], SIDE[0][:, t * COLS:t * COLS + 64], rstd_c[:, t:t + 1],
                                            None, MUL)
            i.then_inc(side_out[0], 1)
            dve.wait_ge(side_out[0], n)
            dt_b = PRM[:, A_DT:A_DT + HEADS].unsqueeze(1).broadcast_to([P, NT, HEADS])
            link(nc.vector.tensor_tensor(gg, bav[:, :, 32:64], dt_b, ADD))
            nc.vector.scalar_tensor_tensor(spl, gg, -1.0, gg, MUL, ALU.max).then_inc(gate_abs, 1)
            dve.wait_ge(gate_exp, 2)
            link(nc.vector.tensor_scalar(bet, bet, 1.0, None, ADD))
            link(nc.vector.reciprocal(bet, bet))
            dve.wait_ge(gate_ln, 1)
            link(nc.vector.scalar_tensor_tensor(gg, gg, 0.0, spl, ALU.max, ADD))
            dve.wait_ge(gate_ea, 1)
            nc.vector.scalar_tensor_tensor(gg, gg, -1.0, eal.unsqueeze(1).broadcast_to([P, NT, HEADS]), MUL, MUL)\
              .then_inc(gate_g, 1)

        def gates2_vector(dve, link, n):
            dve.wait_ge(side_full[0], n)
            nc.vector.tensor_copy(gcl, SIDE[0][:, 0:96]).then_inc(side_out[0], 1)
            dve.wait_ge(side_out[0], n)
            nc.vector.tensor_tensor(kdx, gcl[:, 64:96], gcl[:, 0:32], SUB).then_inc(gate_cum, 1)
            dve.wait_ge(gate_g, 1)
            for t in range(NT):
                nc.vector.tensor_copy(GAg[:, :, 4 * t:4 * t + 4], heads(bet[:, t, :]))
                nc.vector.tensor_copy(GAg[:, :, 8 + 4 * t:12 + 4 * t], heads(gg[:, t, :]))
                nc.vector.tensor_copy(GAg[:, :, 16 + 4 * t:20 + 4 * t], heads(gcl[:, 32 * t:32 * t + 32]))
            dve.wait_ge(gate_fac, 2)
            nc.vector.tensor_copy(GAg[:, :, 28:32], heads(egc))
            nc.vector.tensor_copy(GAg[:, :, 32:36], heads(kdx))
            link(nc.vector.scalar_tensor_tensor(GAg[:, :, 24:28], heads(bet[:, 1, :]), -1.0, heads(egc), MUL, MUL))

        def gdn_step_vector(dve, link, name, p, g, it):
            n = GDN.after(name, it) if p is not None else None
            kind = name[0] if name[1:].isdigit() else name
            side = SIDE[p] if p is not None else None
            if name == "gates1":
                gates1_vector(dve, link, n)
            elif name == "gates2":
                gates2_vector(dve, link, n)
            elif name == "conv_qk0":
                link(nc.vector.tensor_copy(CW[:, :], PRM[:, ds(g * 32 + A_CONV, 32)]))
                dve.wait_ge(side_out[1], GDN.after("qk_t", it))
                conv(link, cq, 0, (0, 1))
            elif name == "conv_qk1":
                conv(link, cq, 0, (2, 3))
            elif name == "conv_v0":
                dve.wait_ge(side_out[1], GDN.after("v_t", it))
                conv(link, cv, 1, (0, 1))
            elif name == "conv_v1":
                conv(link, cv, 1, (2, 3))
            elif name == "ss":
                dve.wait_ge(rb_done, g + 1)
                nc.vector.scalar_tensor_tensor(qkn[:, 0:512], cq[:, 0:512], D_SC, ES[:, 0:512], MUL, MUL)
                nc.vector.tensor_tensor(qkn[:, 512:1024], cq[:, 512:1024], ES[:, 512:1024], MUL).then_inc(qkn_done, 1)
                nc.vector.tensor_copy(GP[:, :], GA[:, ds(g * GW, GW)]).then_inc(gp_ready, 1)
            elif name == "k_t":
                dve.wait_ge(side_full[p], n)
                dve.wait_ge(gp_ready, g + 1)
                for hl in range(4):
                    i = nc.vector.tensor_scalar(kd[:, hl * P:(hl + 1) * P], side[:, (hl // 2) * P:(hl // 2 + 1) * P],
                                                GP[:, 32 + hl:33 + hl], None, MUL)
                i.then_inc(side_out[p], 1)
            elif name == "gb":
                dve.wait_ge(side_full[p], n)
                nc.vector.tensor_tensor(units(E), each(GP[:, 16:24]), units(side[:, :]), SUB).then_inc(side_out[p], 1)
                dve.wait_ge(side_out[p], n)
                nc.vector.tensor_scalar(E, E, 0.0, None, ALU.min).then_inc(dif_done, 1)
            elif name == "kkqk":
                dve.wait_ge(decay_ready, g + 1)
                dve.wait_ge(side_full[p], n)
                for of, buf in ((0, ES), (1, E)):
                    src = units(side[:, of * 512:(of + 1) * 512]).unsqueeze(2).broadcast_to([P, 4, 2, P])
                    b4 = buf.rearrange("p (a b n) -> p a b n", b=2, n=P)
                    i = nc.vector.tensor_tensor(b4, src, b4, MUL)
                i.then_inc(side_out[p], 1)
            elif name == "v_t2":
                dve.wait_ge(side_full[p], n)
                nc.vector.tensor_tensor(units(vb), units(side[:, :]), each(GP[:, 0:8]), MUL).then_inc(side_out[p], 1)
            elif kind in ("t", "u"):
                buf = TR if kind == "t" else UR
                dve.wait_ge(side_full[p], n)
                nc.vector.tensor_tensor(buf[:, :], buf[:, :].bitcast(f32), side[:, :], SUB).then_inc(side_out[p], 1)
            elif name == "nw":
                dve.wait_ge(side_full[p], n)
                link(nc.vector.scalar_tensor_tensor(UF, TR[:, :].bitcast(f32), -1.0, side[:, :], MUL, SUB))
                nc.vector.tensor_tensor(units(YR[:, :]), units(UF), every(K_ID), ADD).then_inc(side_out[p], 1)
            elif name == "ru":
                dve.wait_ge(side_full[p], n)
                nc.vector.tensor_tensor(UF, UR[:, :].bitcast(f32), side[:, :], ADD).then_inc(side_out[p], 1)
            elif name == "ks":
                dve.wait_ge(side_full[p], n)
                nc.vector.tensor_tensor(units(vb[:, 0:512]), units(side[:, 512:1024]), each(GP[:, 28:32], 4), MUL)
                for hl in range(4):
                    part = vb[:, 512 + hl * P:512 + (hl + 1) * P]
                    i = nc.vector.scalar_tensor_tensor(part, side[:, hl * P:(hl + 1) * P], GP[:, 24 + hl:25 + hl], part,
                                                       MUL, ADD)
                i.then_inc(side_out[p], 1)
            elif name == "o":
                dve.wait_ge(side_full[p], n)
                nc.vector.tensor_copy(ES[:, 0:512], side[:, 0:512])
                nc.vector.tensor_tensor(ES[:, 512:1024], side[:, 512:1024], vb[:, 0:512], ADD).then_inc(side_out[p], 1)
            elif name == "osum":
                dve.wait_ge(osq_done, g + 1)
                link(nc.vector.reduce_sum(osum_c, units(N), axis=AX.X))
                nc.vector.tensor_scalar(osum_c, osum_c, 1.0 / P, EPS, MUL, ADD).then_inc(osum_done, 1)
            elif name == "oscale":
                dve.wait_ge(ors_done, g + 1)
                link(nc.vector.tensor_tensor(units(ES), units(ES), each(ors_c), MUL))
                dve.wait_ge(zg_ready, g + 1)
                nc.vector.tensor_tensor(ES, ES, zs, MUL).then_inc(o_scaled, 1)
            elif name == "o_t":
                act_in_vector(dve, p, g + 1)

        def gdn_vector(dve, link, it):
            c, which = gdn_c(it), gdn_which(it)
            for hs in range(32):
                j = hs // 2
                if hs % 2 and (PREP if j < 12 else SOLVE) in which:
                    if j >= 12:
                        add_to_h(dve, c, j, (j + 1) % 2, j - 12)
                    split_lo(dve, c, j + 2)
                    if j > 12 and PREP not in which:
                        norm_vector(dve, NORM1, 1, j - 13, 1)
                for name, p, w_ in steps_at(GDN_STEPS, hs, which):
                    gdn_step_vector(dve, link, name, p, it - 1 if w_ == SOLVE else it, it)
            if PREP not in which:
                norm_vector(dve, NORM1, 1, 3, 1)

        def ffn_vector(dve, ph, base, it, hi0, nxt):
            c = ffn_c(base, it)
            first, final_ = (isinstance(it, int) and it == n for n in (0, FBLK))
            for k in range(12):
                if (k < 8 and final_) or (k >= 8 and first):
                    continue
                if k == 7:
                    dve.wait_ge(acc_out[0], ph.after("gate", it))
                    dve.wait_ge(w_used, c + 8)
                    for t in range(NT):
                        at = slice(t * COLS, (t + 1) * COLS)
                        i = nc.vector.scalar_tensor_tensor(hid[:, at], ACC[1][:, at], rstd_c[:, t:t + 1], sg[:, at],
                                                           MUL, MUL)
                    i.then_inc(acc_out[1], 1)
                if k >= 8:
                    add_to_h(dve, c, k, k % 2, k - 8)
                split_lo(dve, c, k + 2)
                if k > 8 and final_ and nxt:
                    norm_vector(dve, nxt[0], nxt[1], k - 9, nxt[2])
            if not final_:
                act_in_vector(dve, 0, it + (hi0 + 1))
            elif nxt:
                norm_vector(dve, nxt[0], nxt[1], 3, nxt[2])

        def kv_vector(dve):
            for k in range(24):
                split_lo(dve, B_KV, k + 2)

        def compress_vector(dve):
            dve.wait_ge(side_out[0], KV.end["x0"])
            dve.wait_ge(side_out[1], KV.end["x1"])
            dve.wait_ge(w_used, B_CMP)
            for kv in range(2):
                if kv:
                    dve.wait_ge(xp_lo, 1)
                src = kvT[kv].rearrange("p (g n r) -> p g n r", g=KVG, r=16)
                dst = XP[:, 0:CMPB * 60].rearrange("p (h r g n) -> p h r g n", h=2, g=KVG, n=CB)
                for half in range(2):
                    for gq in range(KVG):
                        tok = src[:, gq, half:half + CB, :].rearrange("p n r -> p r n")
                        pos = PRM[:, A_POS + 16 * half:A_POS + 16 * half + 16]
                        i = nc.vector.tensor_tensor(dst[:, half, :, gq, :], tok, each(pos, 16, CB), ADD)
                i.then_inc(xp_done, 1)
                dve.wait_ge(xp_hi, kv + 1)
                at = slice(kv * 2048, kv * 2048 + 1920)
                nc.vector.tensor_tensor(X_LO[:, at], XP[:, 0:1920], X_HI[:, at].bitcast(f32), SUB).then_inc(xp_lo, 1)
            for k in range(8):
                split_lo(dve, B_CMP, k + 2)

        slp, gcol = GP[:, 24:28], GP[:, 0:24]
        sums, mxs, coef, cmx = small[:, 0:24], small[:, 24:32], small[:, 32:40], small[:, 40:48]

        def weigh(dve, link, p, n, b, dst):
            link(nc.vector.reciprocal(coef, sums[:, b[0] * 8:b[0] * 8 + 8]))
            link(nc.vector.tensor_tensor(coef, coef, gcol[:, b[1] * 8:b[1] * 8 + 8], MUL))
            dve.wait_ge(side_full[p], n)
            nc.vector.tensor_tensor(units(dst), units(SIDE[p][:, :]), each(coef), MUL).then_inc(side_out[p], 1)
            dve.wait_ge(side_out[p], n)

        def att_step_vector(dve, link, name, p, g, it):
            n = ATTN.after(name, it)
            b = "ab".find(name[-1])
            if name == "gates":
                dve.wait_ge(side_out[0], n)
                link(nc.vector.tensor_scalar(gsig, gsig, 1.0, None, ADD))
                link(nc.vector.reciprocal(gsig, gsig))
                gv = GA[:, 0:KVG * AW].rearrange("p (g c) -> p g c", c=AW)
                for t in range(NT):
                    for br in range(3):
                        src = gsig[:, t * 48 + br * 16:t * 48 + br * 16 + 16].rearrange("p (g h) -> p g h", h=4)
                        nc.vector.tensor_copy(gv[:, :, br * 8 + t * 4:br * 8 + t * 4 + 4], src)
                link(nc.vector.tensor_copy(gv[:, :, 24:28], K[:, K_SL:K_SL + 16].rearrange("p (g h) -> p g h", h=4)))
            elif name[:2] == "sc" and b >= 0:
                if name == "sc1a":
                    link(nc.vector.tensor_copy(GP[:, 0:AW], GA[:, ds(g * AW, AW)]))
                t = int(name[2])
                sm, wd, dist = (sm1, SEQ, K_D1) if t else (sm0, P, K_D0)
                dve.wait_ge(side_full[p], n)
                for hl in range(4):
                    at = slice(hl * wd, (hl + 1) * wd)
                    i = nc.vector.scalar_tensor_tensor(sm[:, at], K[:, dist:dist + wd], slp[:, hl:hl + 1],
                                                       SIDE[p][:, at], MUL, ADD)
                i.then_inc(side_out[p], 1)
                dve.wait_ge(side_out[p], n)
                mx = mxs[:, 4 * t:4 * t + 4]
                link(nc.vector.reduce_max(mx, units(sm, wd), axis=AX.X))
                nc.vector.tensor_scalar(mx, mx, -1.0, None, MUL).then_inc(mx_done, 1)
            elif name[:2] == "pv" and b >= 0:
                dve.wait_ge(p_exp, g * 4 + 2 * b + 2)
                weigh(dve, link, p, n, (b, b + 1), tmpo if b else oacc)
                if b:
                    link(nc.vector.tensor_tensor(oacc, oacc, tmpo, ADD))
            elif name == "scc":
                for t in range(NT):
                    cd = K[:, K_CD + t * CB:K_CD + (t + 1) * CB].unsqueeze(1).broadcast_to([P, 4, CB])
                    i = nc.vector.tensor_tensor(units(scb, CB)[:, 4 * t:4 * t + 4, :], cd, each(slp, 4, CB), MUL)
                link(i)
                dve.wait_ge(side_full[p], n)
                nc.vector.tensor_tensor(scc, scb, SIDE[p][:, 0:8 * CB], ADD).then_inc(side_out[p], 1)
                dve.wait_ge(side_out[p], n)
                link(nc.vector.reduce_max(cmx, units(scc, CB), axis=AX.X))
                nc.vector.tensor_tensor(units(scc, CB), units(scc, CB), each(cmx, 8, CB), SUB).then_inc(sc_max, 1)
                dve.wait_ge(sc_exp, g + 1)
                link(nc.vector.reduce_sum(sums[:, 16:24], units(scc, CB), axis=AX.X))
                for t in range(NT):
                    seen = K[:, K_CV + t * CB:K_CV + (t + 1) * CB].unsqueeze(1).broadcast_to([P, 4, CB])
                    part = units(scc, CB)[:, 4 * t:4 * t + 4, :]
                    i = nc.vector.tensor_tensor(part, part, seen, MUL)
                i.then_inc(pc_ready, 1)
            elif name == "pvc":
                weigh(dve, link, p, n, (2, 0), tmpo)
                nc.vector.tensor_tensor(oacc, oacc, tmpo, ADD).then_inc(att_done, 1)
            elif name == "o_t":
                act_in_vector(dve, p, g + (GROUPS + FBLK + 1))

        def att_vector(dve, link, it):
            c, which = att_c(it), att_which(it)
            for hs in range(16):
                j = hs // 2
                if hs % 2 and (PROJ if j < 4 else OUT) in which:
                    if j >= 4:
                        add_to_h(dve, c, j, (j + 1) % 2, j - 4)
                    split_lo(dve, c, j + 2)
                    if j > 4 and ATT not in which:
                        norm_vector(dve, NORM4, 4, j - 5, 4)
                for name, p, w_ in steps_at(ATT_STEPS, hs, which):
                    att_step_vector(dve, link, name, p, it - 1 if w_ == ATT else it, it)
            if ATT not in which and OUT in which:
                norm_vector(dve, NORM4, 4, 3, 4)

        def rstd_pool(pool, link, nth):
            pool.wait_ge(sumsq, 2 * nth + 2)
            link(nc.gpsimd.tensor_scalar(rstd_c, sumsq_c, 1.0 / DM, EPS, MUL, ADD))
            link(nc.gpsimd.tensor_tensor(rstd_c, rstd_c, minus_half[:, 0:2], ALU.pow))
            nc.gpsimd.tensor_scalar(SM[:, 6:8], rstd_c, -1.0, None, MUL)
            nc.gpsimd.tensor_scalar(rstd_q, rstd_c, D_SC, None, MUL).then_inc(rstd, 1)

        def gdn_step_pool(pool, link, name, p, g, it):
            kind, lv = name[0], int(name[1:]) if name[1:].isdigit() else None

            def mask(level):
                nc.gpsimd.tensor_tensor(units(NS[level % 2][:, :]), units(N), every(K_LV + level * P), MUL)\
                  .then_inc(ns_ready, 1)

            if name == "ss":
                pool.wait_ge(gp_ready, g + 1)
                nc.gpsimd.tensor_tensor(units(E), each(GP[:, 8:16]), every(K_ONE), MUL).then_inc(gbc_done, 1)
            elif name == "gb":
                pool.wait_ge(qkn_done, g + 1)
                pool.wait_ge(exp_done, g + 1)
                link(nc.gpsimd.tensor_tensor(units(E), units(E), every(K_LOW), MUL))
                link(nc.gpsimd.tensor_tensor(units(ES), units(E), every(K_STR), MUL))
                nc.gpsimd.tensor_tensor(units(ES), units(ES), each(GP[:, 0:8]), MUL).then_inc(decay_ready, 1)
            elif name == "kkqk":
                pool.wait_ge(side_out[1], GDN.after(name, it))
                link(nc.gpsimd.tensor_tensor(units(TR[:, :]), units(ES), every(K_M1), MUL))
                link(nc.gpsimd.tensor_tensor(units(TR[:, :]), units(TR[:, :].bitcast(f32)), every(K_ID), ADD))
            elif name == "lt":
                pool.wait_ge(side_out[1], GDN.after(name, it))
                mask(0)
                link(nc.gpsimd.tensor_tensor(units(UR[:, :]), units(N), every(K_M1T), MUL))
                nc.gpsimd.tensor_tensor(units(UR[:, :]), units(UR[:, :].bitcast(f32)), every(K_ID), ADD)\
                  .then_inc(tu_ready, 1)
                mask(1)
            elif kind == "y" and lv < LEVELS - 2:
                pool.wait_ge(side_full[p], GDN.after(name, it))
                mask(lv + 2)
            elif name == "osum":
                pool.wait_ge(osum_done, g + 1)
                nc.gpsimd.tensor_tensor(ors_c, osum_c, minus_half, ALU.pow).then_inc(ors_done, 1)

        def gdn_pool(pool, link, it):
            which = gdn_which(it)
            for hs in range(32):
                for name, p, w_ in steps_at(GDN_STEPS, hs, which):
                    gdn_step_pool(pool, link, name, p, it - 1 if w_ == SOLVE else it, it)
                if hs == 23 and PREP in which:
                    pool.wait_ge(acc_out[0], GDN.after("in2", it))
                    ong = PRM[:, A_ONG:A_ONG + P].unsqueeze(1).broadcast_to([P, 8, P])
                    nc.gpsimd.tensor_tensor(units(zs), units(zs), ong, MUL).then_inc(zg_ready, 1)

        block = ctx.enter_context(nc.Block())

        @block.sync
        def _(sp):
            for t in range(NT):
                sp.dma_start(H[:, t, :], x[t * P:(t + 1) * P, :]).then_inc(in_const, 16)
            sp.dma_start(K[:, :], consts).then_inc(in_const, 16)
            sp.dma_start(PRM[:, :], params).then_inc(in_const, 16)
            for k in range(RAWS):
                sp.dma_start(RAW[:, k, :], stream[k]).then_inc(raw_full[k], 16)
                if k == 1:
                    sp.dma_start(tailraw, tails[:, 0:KT * 64]).then_inc(tail_in, 16)

            def feed(first, end):
                with sp.Fori(first // RAWS, end // RAWS) as i:
                    for k in range(RAWS):
                        sp.wait_ge(lo_ready, i * RAWS + (k - RAWS + 1))
                        sp.dma_start(RAW[:, k, :], stream[i * RAWS + k]).then_inc(raw_full[k], 16)

            feed(RAWS, B_KV + 8)
            sp.wait_ge(w_used, B_KV)
            sp.wait_ge(sumsq, 6)
            sp.dma_start(w2s, w2).then_inc(w2_in, 16)
            sp.dma_start(tailraw2, tails[:, KT * 64:]).then_inc(tail_in, 16)
            feed(B_KV + 8, B_FFN1 + 8)
            sp.wait_ge(w_used, B_FFN1)
            sp.dma_start(gfs, gfin).then_inc(fin_in, 16)
            feed(B_FFN1 + 8, CHUNKS)
            for t in range(NT):
                sp.wait_ge(y_done, t + 1)
                sp.dma_start(out[t * P:(t + 1) * P, :], hn[:, t, :]).then_inc(out_done, 16)
            sp.wait_ge(out_done, 16 * NT)

        @block.tensor
        def _(pe):
            pe.wait_ge(in_const, 64)
            for r in range(4):
                norm_tensor(pe, NORM0, r, None)
            gdn_tensor(pe, 0)
            with pe.Fori(1, GROUPS) as it:
                gdn_tensor(pe, it)
            gdn_tensor(pe, GROUPS)
            ffn_tensor(pe, FFN0, B_FFN0, NORM1, 0, None)
            with pe.Fori(1, FBLK) as it:
                ffn_tensor(pe, FFN0, B_FFN0, NORM1, it, None)
            ffn_tensor(pe, FFN0, B_FFN0, NORM1, FBLK, NORM2)
            kv_tensor(pe)
            compress_tensor(pe)
            for r in range(4):
                norm_tensor(pe, NORM3, r, None)
            att_tensor(pe, 0)
            att_tensor(pe, 1)
            with pe.Fori(2, KVG) as it:
                att_tensor(pe, it)
            att_tensor(pe, KVG)
            att_tensor(pe, KVG + 1)
            ffn_tensor(pe, FFN1, B_FFN1, NORM4, 0, None)
            with pe.Fori(1, FBLK) as it:
                ffn_tensor(pe, FFN1, B_FFN1, NORM4, it, None)
            ffn_tensor(pe, FFN1, B_FFN1, NORM4, FBLK, None)

        @block.scalar
        def _(act):
            act.wait_ge(in_const, 64)
            split_hi(act, 0, 0)
            for r in range(4):
                norm_scalar(act, NORM0, 0, r, 0)
            split_hi(act, 0, 1)
            squares(act, 0, None, [junk, junk])
            tail_scalar(act, 0, tailraw)
            gdn_scalar(act, 0)
            with act.Fori(1, GROUPS) as it:
                gdn_scalar(act, it)
            gdn_scalar(act, GROUPS)
            ffn_scalar(act, FFN0, B_FFN0, 0, 2, None)
            with act.Fori(1, FBLK) as it:
                ffn_scalar(act, FFN0, B_FFN0, it, 2, None)
            ffn_scalar(act, FFN0, B_FFN0, FBLK, 2, (NORM2, 2, 2))
            kv_scalar(act)
            compress_scalar(act)
            for r in range(4):
                norm_scalar(act, NORM3, 3, r, 3)
            tail_scalar(act, 1, tailraw2)
            att_scalar(act, 0)
            att_scalar(act, 1)
            with act.Fori(2, KVG) as it:
                att_scalar(act, it)
            att_scalar(act, KVG)
            att_scalar(act, KVG + 1)
            ffn_scalar(act, FFN1, B_FFN1, 0, 4, None)
            with act.Fori(1, FBLK) as it:
                ffn_scalar(act, FFN1, B_FFN1, it, 4, None)
            ffn_scalar(act, FFN1, B_FFN1, FBLK, 4, None)
            squares(act, 4, FFN1.end, [hn[:, 0, :], hn[:, 1, :]])

        @block.vector
        def _(dve):
            chain = Chain(dve, dve_chain)
            dve.memset(cin[:, :, 0:3], 0.0).then_inc(pad_zero, 1)
            dve.wait_ge(pad_zero, 1)
            dve.wait_ge(in_const, 64)
            split_lo(dve, 0, 0)
            for r in range(4):
                norm_vector(dve, NORM0, 0, r, 0)
            split_lo(dve, 0, 1)
            tail_vector(dve, 0, tailraw)
            gdn_vector(dve, chain.link, 0)
            chain.loop(1, GROUPS, 16, lambda it: gdn_vector(dve, chain.link, it))
            gdn_vector(dve, chain.link, GROUPS)
            ffn_vector(dve, FFN0, B_FFN0, 0, GROUPS, None)
            with dve.Fori(1, FBLK) as it:
                ffn_vector(dve, FFN0, B_FFN0, it, GROUPS, None)
            ffn_vector(dve, FFN0, B_FFN0, FBLK, GROUPS, (NORM2, 2, 2))
            kv_vector(dve)
            compress_vector(dve)
            for r in range(4):
                norm_vector(dve, NORM3, 3, r, 3)
            tail_vector(dve, 1, tailraw2)
            att_vector(dve, chain.link, 0)
            att_vector(dve, chain.link, 1)
            chain.loop(2, KVG, 15, lambda it: att_vector(dve, chain.link, it))
            att_vector(dve, chain.link, KVG)
            att_vector(dve, chain.link, KVG + 1)
            done = GROUPS + FBLK + KVG
            ffn_vector(dve, FFN1, B_FFN1, 0, done, None)
            with dve.Fori(1, FBLK) as it:
                ffn_vector(dve, FFN1, B_FFN1, it, done, None)
            ffn_vector(dve, FFN1, B_FFN1, FBLK, done, None)
            dve.wait_ge(rstd, 5)
            dve.wait_ge(fin_in, 16)
            for t in range(NT):
                nc.vector.scalar_tensor_tensor(hn[:, t, :], H[:, t, :], rstd_c[:, t:t + 1], gfs, MUL, MUL)\
                  .then_inc(y_done, 1)

        @block.gpsimd
        def _(pool):
            chain = Chain(pool, pool_chain)
            pool.wait_ge(in_const, 64)
            rstd_pool(pool, chain.link, 0)
            gdn_pool(pool, chain.link, 0)
            chain.loop(1, GROUPS, 5, lambda it: gdn_pool(pool, chain.link, it))
            gdn_pool(pool, chain.link, GROUPS)
            for nth in range(1, 5):
                rstd_pool(pool, chain.link, nth)


def constants():
    import numpy as np
    i = np.arange(P)
    K = np.zeros((P, K_END), np.float32)
    K[:, K_ID:K_ID + P] = i[:, None] == i
    K[:, K_TRI:K_TRI + P] = i[:, None] <= i
    K[:, K_ONE:K_ONE + P] = 1.0
    K[:, K_LOW:K_LOW + P] = i <= i[:, None]
    K[:, K_STR:K_STR + P] = i < i[:, None]
    def couples(r, c, n):
        return (r // (2 * n) == c // (2 * n)) & (r % (2 * n) >= n) & (c % (2 * n) < n)
    K[:, K_M1:K_M1 + P] = -1.0 * couples(i[:, None], i, 1)
    K[:, K_M1T:K_M1T + P] = -1.0 * couples(i, i[:, None], 1)
    for lv in range(LEVELS):
        K[:, K_LV + lv * P:K_LV + (lv + 1) * P] = couples(i, i[:, None], 2 << lv)
    FAR = 1e33
    for t in range(NT):
        tok = (t * P + i)[:, None]
        key = np.arange((t + 1) * P)[None]
        at = K_D0 if t == 0 else K_D1
        K[:, at:at + (t + 1) * P] = np.where(key <= tok, tok - key, FAR)
        n = np.arange(CB)[None]
        ok = 16 * n + CMPB - 1 <= tok
        K[:, K_CD + t * CB:K_CD + (t + 1) * CB] = np.where(ok, tok - (16 * n + (CMPB - 1) / 2), FAR)
        K[:, K_CV + t * CB:K_CV + (t + 1) * CB] = ok
    K[:, K_SL:K_SL + 16] = -(2.0 ** (-8.0 * np.arange(1, 17) / 16))
    K[:, K_EPS] = EPS
    K[:, K_NH:] = -0.5
    return K


def layout(inputs):
    import numpy as np
    f = np.ascontiguousarray

    def chunked(wm, kts, c0):
        return [wm[(k0) * P:(k0 + CHK) * P, c0:c0 + COLS].reshape(CHK, P, COLS).transpose(1, 0, 2).reshape(P, CHUNK)
                for k0 in kts]

    win, wout = inputs["gdn_w_in"][0], inputs["gdn_w_out"][0]
    stream = np.empty((CHUNKS, P, CHUNK), np.float32)
    at = 0

    def put(parts):
        nonlocal at
        for q in parts:
            stream[at] = q
            at += 1

    allk = range(0, KT, CHK)
    QK = 16 * P
    for g in range(GROUPS + 1):
        if g < GROUPS:
            qk = np.concatenate([win[:, 256 * g:256 * g + 256], win[:, QK + 256 * g:QK + 256 * g + 256]], 1)
            put(chunked(qk, allk, 0))
            put(chunked(win, allk, 2 * QK + COLS * g))
            put(chunked(win, allk, 4 * QK + COLS * g))
        if g:
            for c in range(4):
                put(chunked(wout, [4 * (g - 1)], c * COLS))

    def ffn(l):
        gu, dn = inputs["ffn_w_gate_up"][l], inputs["ffn_w_down"][l]
        for j in range(FBLK + 1):
            if j < FBLK:
                put(chunked(gu, allk, j * COLS))
                put(chunked(gu, allk, FFN_H + j * COLS))
            if j:
                for c in range(4):
                    put(chunked(dn, [4 * (j - 1)], c * COLS))

    ffn(0)
    for c in range(6):
        put(chunked(inputs["kv_w"], allk, c * COLS))
    for wm in (inputs["cmp_w1_k"], inputs["cmp_w1_v"]):
        for c in range(4):
            put([wm[c * 1024:(c + 1) * 1024].reshape(8, P, 256).transpose(1, 0, 2).reshape(P, CHUNK)])
    nin, nout = inputs["nsa_w_in"][0], inputs["nsa_w_out"][0]
    for it in range(KVG + 2):
        if it < KVG:
            put(chunked(nin, allk, it * COLS))
        if it >= 2:
            for c in range(4):
                put(chunked(nout, [4 * (it - 2)], c * COLS))
    ffn(1)
    assert at == CHUNKS

    prm = np.empty((P, A_END), np.float32)
    cw = inputs["gdn_conv_w"][0]
    for g in range(GROUPS):
        for nth in range(2):
            for b in range(4):
                c0 = (256 * g + b * P if b < 2 else QK + 256 * g + (b - 2) * P) if nth == 0 else 2 * QK + COLS * g + b * P
                col = A_CONV + g * 32 + nth * 16 + b * 4
                prm[:, col:col + 4] = cw[:, c0:c0 + P].T
    gains = [inputs["mixer_norm_g"][0], inputs["ffn_norm_g"][0], inputs["kv_norm_g"], inputs["mixer_norm_g"][1],
             inputs["ffn_norm_g"][1]]
    for n, gv in enumerate(gains):
        prm[:, A_GAIN + n * KT:A_GAIN + (n + 1) * KT] = gv.reshape(KT, P).T
    prm[:, A_ALOG:A_ALOG + HEADS] = inputs["gdn_a_log"][0][None]
    prm[:, A_DT:A_DT + HEADS] = inputs["gdn_dt_bias"][0][None]
    prm[:, A_ONG:A_ONG + P] = inputs["gdn_out_norm_g"][0][None]
    prm[:, A_POS:A_POS + CMPB] = inputs["cmp_pos"].T
    tails = np.concatenate([win[:, 6 * QK:].reshape(KT, P, 64).transpose(1, 0, 2).reshape(P, -1),
                            nin[:, 2048:].reshape(KT, P, 48).transpose(1, 0, 2).reshape(P, -1)], 1)
    w2 = np.concatenate([inputs[n].reshape(2, P, P).transpose(1, 0, 2).reshape(P, 256)
                         for n in ("cmp_w2_k", "cmp_w2_v")], 1)
    gfin = np.repeat(inputs["final_norm_g"][None], P, 0)
    return {"stream": stream, "consts": constants(), "params": prm, "tails": f(tails), "w2": f(w2), "gfin": f(gfin),
            "x": f(inputs["x"][0])}


def kernel(**inputs):
    import numpy as np
    import concourse.bacc as bacc
    from concourse.bass_utils import run_bass_kernel_spmd

    arrays = layout({k: np.asarray(v) for k, v in inputs.items()})
    nc = bacc.Bacc("TRN2", target_bir_lowering=False, num_devices=1)
    args = [nc.dram_tensor(k, a.shape, mybir.dt.float32, kind="ExternalInput").ap() for k, a in arrays.items()]
    out = nc.dram_tensor("out", (SEQ, DM), mybir.dt.float32, kind="ExternalOutput").ap()
    build(nc, *args, out)
    r = run_bass_kernel_spmd(nc, [arrays], core_ids=[0])
    return r.results[0]["out"].reshape(1, SEQ, DM)
```

```python
import concourse.bass as bass
from concourse import mybir
from contextlib import ExitStack

P = 128
SEQ, DM = 256, 2048
NT = SEQ // P
KT = DM // P
COLS = 512
CHK = 4
CHUNK = CHK * COLS
PIECE = CHUNK // 2
WS = 4
HEADS = 32
GROUPS = 8
FFN_H = 5632
FBLK = FFN_H // COLS
KVG = 4
CB = 15
CMPB = 32
EPS = 1e-6
RAWS = 4
LEVELS = 6
C_GDN = 16 * GROUPS
C_FFN = 12 * FBLK
C_KV, C_CMP, C_ATT = 24, 8, 32
B_FFN0 = C_GDN
B_KV = B_FFN0 + C_FFN
B_CMP = B_KV + C_KV
B_ATT = B_CMP + C_CMP
B_FFN1 = B_ATT + C_ATT
CHUNKS = B_FFN1 + C_FFN

K_ID, K_TRI, K_ONE, K_LOW, K_STR, K_M1, K_M1T, K_LV = [P * i for i in range(8)]
K_D0 = K_LV + LEVELS * P
K_D1 = K_D0 + P
K_CD = K_D1 + 2 * P
K_CV = K_CD + NT * CB
K_SL = K_CV + NT * CB
K_EPS = K_SL + 16
K_NH = K_EPS + 1
K_END = K_NH + 8
A_CONV, A_GAIN = 0, GROUPS * 32
A_ALOG = A_GAIN + 5 * KT
A_DT = A_ALOG + HEADS
A_ONG = A_DT + HEADS
A_POS = A_ONG + P
A_END = A_POS + CMPB
GW = 36
AW = 28

PREP, SOLVE, OUT, ONCE = "prep", "solve", "out", "once"
GDN_PART = {0: "qk", 2: "v", 3: "z"}
GDN_ACC = {"qk": 0, "v": 0, "z": 1}
GDN_STEPS = [
    (7, "gates1", 0, ONCE),
    (0, "y0", 0, SOLVE), (1, "t0", 1, SOLVE), (1, "u0", 0, SOLVE),
    (2, "y1", 0, SOLVE), (3, "t1", 1, SOLVE), (3, "u1", 0, SOLVE),
    (4, "y2", 0, SOLVE), (5, "t2", 1, SOLVE), (5, "u2", 0, SOLVE),
    (6, "y3", 0, SOLVE), (7, "t3", 1, SOLVE), (7, "u3", 0, SOLVE),
    (12, "gates2", 0, ONCE),
    (8, "y4", 0, SOLVE), (9, "t4", 1, SOLVE), (9, "u4", 0, SOLVE), (10, "qk_t", 1, PREP),
    (10, "y5", 0, SOLVE), (11, "conv_qk0", None, PREP), (11, "t5", 1, SOLVE), (11, "u5", 0, SOLVE),
    (12, "nw", 1, SOLVE), (13, "ru", 0, SOLVE), (14, "v0", 1, SOLVE), (15, "conv_qk1", None, PREP),
    (15, "s", 0, SOLVE), (16, "ks", 1, SOLVE), (17, "v1", 0, SOLVE), (18, "o", 0, SOLVE), (19, "osum", None, SOLVE),
    (19, "factors", None, PREP), (20, "oscale", None, SOLVE), (21, "gb", 0, PREP), (21, "o_t", 1, SOLVE),
    (20, "silu_qk", None, PREP), (22, "squares", None, PREP), (23, "ss", 0, PREP), (25, "v_t", 1, PREP),
    (25, "k_t", 0, PREP), (26, "conv_v0", None, PREP), (27, "kkqk", 1, PREP), (27, "conv_v1", None, PREP),
    (30, "silu_v", None, PREP), (29, "lt", 1, PREP), (30, "at", 0, PREP), (31, "v_t2", 0, PREP)]
GDN_STEPS.sort(key=lambda e: e[0])

PROJ, ATT = "proj", "att"
ATT_STEPS = [
    (7, "gates", 0, ONCE),
    (0, "sc1a", 0, ATT), (0, "sc0a", 1, ATT), (2, "pt1a", 0, ATT), (2, "pt0a", 1, ATT), (4, "pva", 0, ATT),
    (5, "sc1b", 0, ATT), (5, "sc0b", 1, ATT), (7, "pt1b", 0, ATT), (7, "pt0b", 1, ATT), (9, "pvb", 0, ATT),
    (9, "scc", 1, ATT), (11, "ptc", 0, ATT), (13, "pvc", 1, ATT),
    (15, "o_t", 0, ATT), (15, "q_t", 1, PROJ)]
ATT_STEPS.sort(key=lambda e: e[0])


def steps_at(table, hs, which):
    return [(n, p, w) for h, n, p, w in table if h == hs and w in which]


class Phase:

    def __init__(self, start, lists, lo=0, hi=0, body=()):
        self.start, self.lo, self.hi = dict(start), lo, hi
        self.per = {k: sum(q == k for q, _ in body) for k in start}
        self.base, self.index = {}, {}
        n = dict(start)
        its = sorted([i for i in lists if i < lo]) + (["body"] if hi > lo else []) + sorted(i for i in lists if i >= hi)
        for i in its:
            self.base[i] = dict(n)
            seen = {k: 0 for k in n}
            self.index[i] = {}
            for pair, name in (body if i == "body" else lists[i]):
                self.index[i][name] = (pair, seen[pair])
                seen[pair] += 1
            times = hi - lo if i == "body" else 1
            n = {k: n[k] + times * seen[k] for k in n}
        self.end = n

    def before(self, name, it):
        key = it if isinstance(it, int) and it in self.base else "body"
        pair, at = self.index[key][name]
        value = self.base[key][pair] + at
        return value if key != "body" else (it - self.lo) * self.per[pair] + value

    def after(self, name, it):
        return self.before(name, it) + 1


def gdn_uses(which):
    uses = []
    for hs in range(32):
        j = hs // 2
        if hs % 8 == 7 and j // 4 != 1 and PREP in which:
            part = GDN_PART[j // 4]
            uses.append((f"a{GDN_ACC[part]}", part))
        if hs % 2 and j // 4 == 1 and OUT in which:
            uses.append((f"a{(j + 1) % 2}", f"out{j - 4}"))
        uses += [(f"x{p}", n) for n, p, _ in steps_at(GDN_STEPS, hs, which) if p is not None]
    return uses


def ffn_uses(up, down):
    uses = [("a0", "gate"), ("a1", "up")] if up else []
    uses += [(f"a{k % 2}", f"down{k}") for k in range(4)] if down else []
    return uses + ([("x0", "hid_t")] if up else [])


def att_uses(which):
    uses = []
    for hs in range(16):
        if hs == 7 and PROJ in which:
            uses.append(("a0", "q"))
        if hs % 2 and hs >= 9 and OUT in which:
            uses.append((f"a{(hs // 2 + 1) % 2}", f"out{hs // 2 - 4}"))
        uses += [(f"x{p}", n) for n, p, _ in steps_at(ATT_STEPS, hs, which)]
    return uses


NORM_USES = [(f"x{r % 2}", f"norm{r}") for r in range(4)]
KV_TURNED = (0, 1, 2, 4)
KV_USES = []
for _k in range(6):
    KV_USES.append((f"a{_k % 2}", f"kv{_k}"))
    if _k in KV_TURNED:
        KV_USES.append((f"x{_k % 2}", f"kv_t{_k}"))
CMP_USES = [("a0", "hid0"), ("a1", "hid1"), ("x0", "hid_t"), ("x1", "w2")]

ZERO = {"a0": 0, "a1": 0, "x0": 0, "x1": 0}
NORM0 = Phase(ZERO, {0: NORM_USES})
GDN = Phase(NORM0.end, {0: gdn_uses((PREP, ONCE)), 1: gdn_uses((PREP, SOLVE)), GROUPS: gdn_uses((SOLVE, OUT)),
                        GROUPS + 1: gdn_uses((OUT,))}, 2, GROUPS, gdn_uses((PREP, SOLVE, OUT)))
NORM1 = Phase(GDN.end, {0: NORM_USES})
FFN0 = Phase(NORM1.end, {0: ffn_uses(True, False), FBLK: ffn_uses(False, True)}, 1, FBLK, ffn_uses(True, True))
NORM2 = Phase(FFN0.end, {0: NORM_USES})
KV = Phase(NORM2.end, {0: KV_USES})
CMP = Phase(KV.end, {0: CMP_USES})
NORM3 = Phase(CMP.end, {0: NORM_USES})
ATTN = Phase(NORM3.end, {0: att_uses((PROJ, ONCE)), 1: att_uses((PROJ, ATT)), 4: att_uses((ATT, OUT)),
                         5: att_uses((OUT,))}, 2, KVG, att_uses((PROJ, ATT, OUT)))
NORM4 = Phase(ATTN.end, {0: NORM_USES})
FFN1 = Phase(NORM4.end, {0: ffn_uses(True, False), FBLK: ffn_uses(False, True)}, 1, FBLK, ffn_uses(True, True))


class Chain:

    def __init__(self, eng, semaphore):
        self.eng, self.sem, self.n, self.seen = eng, semaphore, 0, 0

    def link(self, instruction):
        instruction.then_inc(self.sem, 1)
        self.n, self.seen = self.n + 1, self.seen + 1
        self.eng.wait_ge(self.sem, self.n)

    def loop(self, lo, hi, per, body):
        base = self.n
        with self.eng.Fori(lo, hi) as it:
            self.n, self.seen = (it - lo) * per + base, 0
            body(it)
            assert self.seen == per, (self.seen, per)
        self.n = base + (hi - lo) * per


def build(nc, stream, consts, params, tails, w2, gfin, x, out):
    f32, f32r = mybir.dt.float32, mybir.dt.float32r
    ALU, ACT, AX = mybir.AluOpType, mybir.ActivationFunctionType, mybir.AxisListType
    MUL, ADD, SUB = ALU.mult, ALU.add, ALU.subtract
    ds = bass.ds
    D_SC = float(P) ** -0.5
    ONE = dict(start=True, stop=True)
    ctx = ExitStack()

    def sb(name, shape, dt=f32):
        return ctx.enter_context(nc.sbuf_tensor(name, shape, dt))

    def sem(name):
        return ctx.enter_context(nc.semaphore(name))

    def psum(name):
        return ctx.enter_context(nc.psum_tensor(name, [P, NT * COLS], f32))

    with ctx:
        RAW = sb("RAW", [P, RAWS, CHUNK])
        W_HI, W_LO = (sb(n, [P, WS, PIECE], f32r) for n in ("W_HI", "W_LO"))
        X_HI, X_LO = (sb(n, [P, KT * SEQ], f32r) for n in ("X_HI", "X_LO"))
        A_HI, A_LO = (sb(n, [P, CHK * SEQ], f32r) for n in ("A_HI", "A_LO"))
        H = sb("H", [P, NT, DM])
        K, PRM = sb("K", [P, K_END]), sb("PRM", [P, A_END])
        GA, GP, CW, SM = sb("GA", [P, GROUPS * GW]), sb("GP", [P, GW]), sb("CW", [P, 32]), sb("SM", [P, 24])
        TR, UR, YR, NS0, NS1 = (sb(n, [P, 1024], f32r) for n in ("TR", "UR", "YR", "NS0", "NS1"))
        NS = [NS0, NS1]
        WORK = sb("WORK", [P, 13 * 1024 + 384])
        ACC = [psum(f"ACC{i}") for i in range(2)]
        SIDE = [psum(f"SIDE{i}") for i in range(2)]

        def w(off, n):
            return WORK[:, off:off + n]

        def tiles2(ap):
            return ap.rearrange("p (t n) -> p t n", t=NT)

        def units(ap, n=P):
            return ap.rearrange("p (u n) -> p u n", n=n)

        def each(cols, n=8, width=P):
            return cols.unsqueeze(2).broadcast_to([P, n, width])

        def every(at, n=8):
            return K[:, at:at + P].unsqueeze(1).broadcast_to([P, n, P])

        ident, tri, ones = K[:, K_ID:K_ID + P], K[:, K_TRI:K_TRI + P], K[:, K_ONE:K_ONE + P]
        eps_col, minus_half = K[:, K_EPS:K_EPS + 1], K[:, K_NH:K_NH + 8]
        sumsq_c, rstd_c, rstd_q = SM[:, 0:2], SM[:, 2:4], SM[:, 4:6]
        osum_c, ors_c = SM[:, 8:16], SM[:, 16:24]

        tokraw = w(0, 1024)
        cin = WORK[:, 1024:1024 + 4 * 259].rearrange("p (b n) -> p b n", n=259)
        cq, cv, qkn, vb, E, ES, N, AT, UF, zs = [w(2064 + 1024 * i, 1024) for i in range(10)]
        S, kd = w(2064 + 10240, 512), w(2064 + 10752, 512)
        tailraw = w(7 * 1024, 1024)
        junk = w(8 * 1024, DM)
        sg, hid = w(0, 1024), w(1024, 1024)
        kcT, vc = w(0, 64), WORK[0:CB, 64:576]
        kT = [w(576, 1024), w(1600, 1024)]
        vS = [w(2624, 1024), w(3648, 1024)]
        b0 = 4672
        tkv, kvT = [w(b0, 1024), w(b0 + 1024, 1024)], [w(b0 + 2048, 1024), w(b0 + 3072, 1024)]
        KV_TO = {0: kvT[0], 1: kvT[1], 2: kT[0], 4: kT[1]}
        XP, hc, hcT = w(b0 + 4096, 2048), w(b0 + 6144, 512), w(b0 + 6656, 256)
        w2s, tailraw2 = w(b0 + 7168, 512), w(b0 + 7680, KT * 48)
        qtok, qT, sm1, p1T, oacc, tmpo = [w(b0 + 1024 * i, 1024) for i in range(6)]
        sm0, p0T = w(b0 + 6144, 512), w(b0 + 6656, 512)
        pcT = WORK[0:CB, b0 + 7168:b0 + 8192]
        scc, scb, small = w(b0 + 8192, 120), w(b0 + 8320, 120), w(b0 + 8448, 64)
        gsig = w(b0 + 8512, 96)
        hn = tiles2(w(8 * 1024, NT * DM))
        gfs = w(2 * 1024, DM)

        (in_head, in_const, tail_in, w2_in, fin_in, pad_zero, hi_ready, lo_ready, w_used, x_hi, sumsq, rstd, tail_hi, tail_lo,
         gate_abs, gate_exp, gate_ea, gate_ln, gate_g, gate_cum, gate_fac, conv_done, silu_done, sq_done, rb_done,
         qkn_done, gp_ready, gbc_done, dif_done, exp_done, decay_ready, tu_ready, ns_ready, osq_done, osum_done,
         ors_done, o_scaled, zg_ready, act_hi, xp_done, xp_hi, xp_lo, mx_done, p_exp, sc_max, sc_exp, pc_ready,
         att_done, y_done, out_done, dve_chain, pool_chain) = (sem(n) for n in (
             "in_head in_const tail_in w2_in fin_in pad_zero hi_ready lo_ready w_used x_hi sumsq rstd tail_hi tail_lo "
             "gate_abs gate_exp gate_ea gate_ln gate_g gate_cum gate_fac conv_done silu_done sq_done rb_done "
             "qkn_done gp_ready gbc_done dif_done exp_done decay_ready tu_ready ns_ready osq_done osum_done "
             "ors_done o_scaled zg_ready act_hi xp_done xp_hi xp_lo mx_done p_exp sc_max sc_exp pc_ready "
             "att_done y_done out_done dve_chain pool_chain").split())
        x_in = [sem(f"x_in{i}") for i in range(4)]
        raw_full = [sem(f"raw_full{i}") for i in range(RAWS)]
        acc_out = [sem(f"acc_out{i}") for i in range(2)]
        side_full = [sem(f"side_full{i}") for i in range(2)]
        side_out = [sem(f"side_out{i}") for i in range(2)]

        def wait_past(eng, semaphore, n):
            if not (isinstance(n, int) and n == 0):
                eng.wait_ge(semaphore, n)

        def gdn_c(it, hs):
            if not isinstance(it, int):
                return it * 32 - 16
            return {0: 0, 1: 24, GROUPS: 32 * GROUPS - 24, GROUPS + 1: 32 * GROUPS - 16}[it] - (8 if it < 2 and hs >= 16 else 0)

        def ffn_c(base, it):
            return {0: 2 * base, FBLK: 2 * base + 24 * (FBLK - 1)}[it] if isinstance(it, int) else it * 24 + (2 * base - 8)

        def att_c(it):
            return 2 * B_ATT + {0: 0, 1: 8, 4: 40, 5: 48}[it] if isinstance(it, int) else it * 16 + (2 * B_ATT - 16)

        def gdn_which(it):
            some = {0: (PREP, ONCE), 1: (PREP, SOLVE), GROUPS: (SOLVE, OUT), GROUPS + 1: (OUT,)}
            return some[it] if isinstance(it, int) else (PREP, SOLVE, OUT)

        def gdn_section(j, which):
            return (OUT if j // 4 == 1 else PREP) in which

        def att_which(it):
            every_ = (PROJ, ATT, OUT)
            return {0: (PROJ, ONCE), 1: (PROJ, ATT), 4: (ATT, OUT), 5: (OUT,)}[it] if isinstance(it, int) else every_

        def raw_piece(h):
            return RAW[:, h // 2 % RAWS, h % 2 * PIECE:(h % 2 + 1) * PIECE]

        def products(pe, c, h, acc, hi, lo, first, last, base=0):
            pe.wait_ge(lo_ready, c + (h + 1))
            for q in range(2):
                for t in range(NT):
                    dst = ACC[acc][:, t * COLS:(t + 1) * COLS]
                    at = (base + 2 * (h % 2) + q) * SEQ + t * P
                    wh, wl = (b[:, h % WS, q * COLS:(q + 1) * COLS] for b in (W_HI, W_LO))
                    nc.tensor.matmul(dst, hi[:, at:at + P], wh, start=first and h % 2 == 0 and q == 0, stop=False)
                    nc.tensor.matmul(dst, hi[:, at:at + P], wl, start=False, stop=False)
                    m = nc.tensor.matmul(dst, lo[:, at:at + P], wh, start=False, stop=last and h % 2 == 1 and q == 1)
            m.then_inc(w_used, 1)

        def turn(pairs, p):
            for to, src in pairs:
                m = nc.tensor.transpose(SIDE[p][:, to:to + P], src, ident)
            m.then_inc(side_full[p], 1)

        def by_block(buf):
            return [((b * NT + t) * P, buf[:, t * COLS + b * P:t * COLS + (b + 1) * P])
                    for b in range(4) for t in range(NT)]

        def by_unit(buf):
            return [((hl * NT + t) * P, buf[:, (t * 4 + hl) * P:(t * 4 + hl + 1) * P])
                    for t in range(NT) for hl in range(4)]

        def norm_tensor(pe, norm, r, ready):
            wait_past(pe, side_out[r % 2], norm.before(f"norm{r}", 0))
            if ready:
                pe.wait_ge(acc_out[ready[0]], ready[1])
            turn([((q * NT + t) * P, H[:, t, (4 * r + q) * P:(4 * r + q + 1) * P]) for q in range(4)
                  for t in range(NT)], r % 2)

        def tail_tensor(pe, nth, n, width):
            wait_past(pe, side_out[0], n)
            pe.wait_ge(tail_lo, nth + 1)
            for t in range(NT):
                dst = SIDE[0][:, t * COLS:t * COLS + width]
                for kt in range(KT):
                    at = kt * SEQ + t * P
                    wh, wl = (b[:, kt * width:(kt + 1) * width] for b in (A_HI, A_LO))
                    nc.tensor.matmul(dst, X_HI[:, at:at + P], wh, start=kt == 0, stop=False)
                    nc.tensor.matmul(dst, X_HI[:, at:at + P], wl, start=False, stop=False)
                    m = nc.tensor.matmul(dst, X_LO[:, at:at + P], wh, start=False, stop=kt == KT - 1)
            m.then_inc(side_full[0], 1)

        def unit_products(p, lhs, rhs, n=8, at=0):
            for u in range(n):
                m = nc.tensor.matmul(SIDE[p][:, u * P:(u + 1) * P], lhs[:, at + u * P:at + (u + 1) * P],
                                     rhs[:, u * P:(u + 1) * P], **ONE)
            m.then_inc(side_full[p], 1)

        def gdn_step_tensor(pe, name, p, g, it):
            if p is None:
                return
            wait_past(pe, side_out[p], GDN.before(name, it))
            dst = SIDE[p]
            kind, lv = name[0], int(name[1:]) if name[1:].isdigit() else None
            if name == "gates1":
                tail_tensor(pe, 0, 0, 64)
            elif name == "gates2":
                pe.wait_ge(in_const, 16)
                pe.wait_ge(gate_g, 1)
                for t in range(NT):
                    nc.tensor.matmul(dst[:, 32 * t:32 * t + 32], tri, gg[:, t, :], **ONE)
                nc.tensor.matmul(dst[:, 64:96], ones, gg[:, 0, :], **ONE).then_inc(side_full[0], 1)
            elif name == "qk_t":
                pe.wait_ge(acc_out[0], GDN.after("qk", it))
                turn(by_block(tokraw), p)
            elif name == "v_t":
                pe.wait_ge(acc_out[0], GDN.after("v", it))
                turn(by_block(tokraw), p)
            elif name == "ss":
                pe.wait_ge(sq_done, g + 1)
                for i in range(2):
                    m = nc.tensor.matmul(dst[:, i * 512:(i + 1) * 512], ones, ES[:, i * 512:(i + 1) * 512], **ONE)
                m.then_inc(side_full[p], 1)
            elif name == "k_t":
                pe.wait_ge(qkn_done, g + 1)
                turn([(hq * P, qkn[:, 512 + hq * SEQ:512 + hq * SEQ + P]) for hq in range(2)], p)
            elif name == "gb":
                pe.wait_ge(gbc_done, g + 1)
                for u in range(8):
                    m = nc.tensor.matmul(dst[:, u * P:(u + 1) * P], E[:, u * P:(u + 1) * P], tri, **ONE)
                m.then_inc(side_full[p], 1)
            elif name == "kkqk":
                pe.wait_ge(qkn_done, g + 1)
                for of in range(2):
                    for t in range(NT):
                        for hq in range(2):
                            a = hq * SEQ + t * P
                            kk = qkn[:, 512 + a:512 + a + P]
                            to = of * 512 + (t * 2 + hq) * P
                            m = nc.tensor.matmul(dst[:, to:to + P], qkn[:, a:a + P] if of else kk, kk, **ONE)
                m.then_inc(side_full[p], 1)
            elif name == "v_t2":
                pe.wait_ge(silu_done, 2 * g + 2)
                turn([((t * 4 + hl) * P, cv[:, hl * SEQ + t * P:hl * SEQ + (t + 1) * P])
                      for t in range(NT) for hl in range(4)], p)
            elif name in ("lt", "at"):
                pe.wait_ge(side_out[1], GDN.after("kkqk", it))
                src = ES if name == "lt" else E
                turn([(u * P, src[:, u * P:(u + 1) * P]) for u in range(8)], p)
            elif kind == "y":
                pe.wait_ge(ns_ready, g * LEVELS + lv + 1)
                if lv == 0:
                    pe.wait_ge(tu_ready, g + 1)
                else:
                    pe.wait_ge(side_out[1], GDN.after(f"t{lv - 1}", it))
                unit_products(p, NS[lv % 2], TR)
            elif kind == "t":
                pe.wait_ge(side_out[0], GDN.after(f"y{lv}", it))
                unit_products(p, UR, YR)
            elif kind == "u":
                unit_products(p, YR, UR)
            elif name == "nw":
                pe.wait_ge(side_out[1], GDN.after("t5", it))
                unit_products(p, N, TR[:, :].bitcast(f32))
            elif name == "ru":
                pe.wait_ge(side_out[1], GDN.after("nw", it))
                unit_products(p, YR, UR)
            elif name == "v0":
                pe.wait_ge(side_out[0], GDN.after("ru", it))
                unit_products(p, UF, vb, 4)
            elif name == "s":
                pe.wait_ge(side_out[1], GDN.after("v0", it))
                unit_products(p, kd, E, 4)
            elif name == "ks":
                pe.wait_ge(side_out[0], GDN.after("s", it))
                for of in range(2):
                    for hq in range(2):
                        a = (0 if of else 512) + hq * SEQ + P
                        m = nc.tensor.matmul(dst[:, of * 512 + hq * SEQ:of * 512 + (hq + 1) * SEQ], qkn[:, a:a + P],
                                             S[:, hq * SEQ:(hq + 1) * SEQ], **ONE)
                m.then_inc(side_full[p], 1)
            elif name == "v1":
                pe.wait_ge(side_out[1], GDN.after("ks", it))
                unit_products(p, UF, vb[:, 512:1024], 4, 512)
            elif name == "o":
                pe.wait_ge(side_out[0], GDN.after("v1", it))
                unit_products(p, AT, E)
            elif name == "o_t":
                pe.wait_ge(o_scaled, g + 1)
                turn(by_unit(ES), p)

        def gdn_tensor(pe, it):
            which = gdn_which(it)
            for hs in range(32):
                j, half, c = hs // 2, hs % 2, gdn_c(it, hs)
                if j // 4 != 1 and PREP in which:
                    part, k = GDN_PART[j // 4], j % 4
                    acc = GDN_ACC[part]
                    if half == 0 and k == 0:
                        wait_past(pe, acc_out[acc], GDN.before(part, it))
                    if half == 0 and ONCE in which and j < 4:
                        pe.wait_ge(side_out[j % 2], NORM0.after(f"norm{j}", 0))
                    products(pe, c, hs, acc, X_HI, X_LO, k == 0, k == 3, 4 * k)
                if j // 4 == 1 and OUT in which:
                    acc = (j + 1) % 2
                    if half == 0:
                        pe.wait_ge(acc_out[acc], GDN.before(f"out{j - 4}", it))
                        if j == 4:
                            pe.wait_ge(side_out[1], GDN.after("o_t", it - 1))
                    products(pe, c, hs, acc, A_HI, A_LO, True, True)
                    if half and j > 4 and SOLVE not in which:
                        norm_tensor(pe, NORM1, j - 5, ((j - 5 + 1) % 2, GDN.after(f"out{j - 5}", it)))
                for name, p, w_ in steps_at(GDN_STEPS, hs, which):
                    gdn_step_tensor(pe, name, p, it - 1 if w_ == SOLVE else it, it)
            if which == (OUT,):
                norm_tensor(pe, NORM1, 3, (0, GDN.after("out3", it)))

        def ffn_tensor(pe, ph, base, norm, it, nxt):
            c = ffn_c(base, it)
            first = isinstance(it, int) and it == 0
            final_ = isinstance(it, int) and it == FBLK
            for k in range(12):
                if k < 8 and not final_:
                    if k % 4 == 0:
                        pe.wait_ge(acc_out[k // 4], ph.before("up" if k else "gate", it))
                    if first and k < 4:
                        pe.wait_ge(side_out[k % 2], norm.after(f"norm{k}", 0))
                    for half in range(2):
                        products(pe, c, 2 * k + half, k // 4, X_HI, X_LO, k % 4 == 0, k % 4 == 3, 4 * (k % 4))
                if k >= 8 and not first:
                    pe.wait_ge(acc_out[k % 2], ph.before(f"down{k - 8}", it))
                    if k == 8:
                        pe.wait_ge(side_out[0], ph.before("hid_t", it) if not final_ else ph.end["x0"])
                    for half in range(2):
                        products(pe, c, 2 * k + half, k % 2, A_HI, A_LO, True, True)
                    if final_ and nxt and k > 8:
                        norm_tensor(pe, nxt, k - 9, ((k - 9) % 2, ph.after(f"down{k - 9}", it)))
            if not final_:
                pe.wait_ge(side_out[0], ph.before("hid_t", it))
                pe.wait_ge(acc_out[1], ph.after("up", it))
                turn(by_block(hid), 0)
            elif nxt:
                norm_tensor(pe, nxt, 3, (1, ph.after("down3", it)))

        def kv_tensor(pe):
            for s in range(6):
                acc = s % 2
                pe.wait_ge(acc_out[acc], KV.before(f"kv{s}", 0))
                for k in range(4):
                    if s == 0:
                        pe.wait_ge(side_out[k % 2], NORM2.after(f"norm{k}", 0))
                    for half in range(2):
                        products(pe, 2 * B_KV, 8 * s + 2 * k + half, acc, X_HI, X_LO, k == 0, k == 3, 4 * k)
                    if k == 0 and s - 1 in KV_TURNED:
                        pe.wait_ge(side_out[1 - acc], KV.before(f"kv_t{s - 1}", 0))
                        pe.wait_ge(acc_out[1 - acc], KV.after(f"kv{s - 1}", 0))
                        turn(by_block(tkv[1 - acc]), 1 - acc)

        def compress_tensor(pe):
            for kv in range(2):
                pe.wait_ge(xp_lo, kv + 1)
                pe.wait_ge(acc_out[kv], CMP.before(f"hid{kv}", 0))
                for k in range(8):
                    h = 8 * kv + k
                    pe.wait_ge(lo_ready, 2 * B_CMP + h + 1)
                    for q in range(4):
                        at = kv * 2048 + (4 * k + q) * 60
                        wh, wl = (b[:, h % WS, q * 256:(q + 1) * 256] for b in (W_HI, W_LO))
                        d = ACC[kv][:, 0:256]
                        nc.tensor.matmul(d, X_HI[:, at:at + P], wh, start=k == 0 and q == 0, stop=False)
                        nc.tensor.matmul(d, X_HI[:, at:at + P], wl, start=False, stop=False)
                        m = nc.tensor.matmul(d, X_LO[:, at:at + P], wh, start=False, stop=k == 7 and q == 3)
                    m.then_inc(w_used, 1)
            for kv in range(2):
                pe.wait_ge(acc_out[kv], CMP.after(f"hid{kv}", 0))
            pe.wait_ge(side_out[0], CMP.before("hid_t", 0))
            for i in range(4):
                m = nc.tensor.transpose(SIDE[0][:, i * 64:i * 64 + 60], hc[0:60, i * P:(i + 1) * P],
                                        K[0:60, K_ID:K_ID + 60])
            m.then_inc(side_full[0], 1)
            pe.wait_ge(side_out[1], CMP.before("w2", 0))
            pe.wait_ge(side_out[0], CMP.after("hid_t", 0))
            pe.wait_ge(w2_in, 16)
            for kt in range(2):
                nc.tensor.matmul(SIDE[1][:, 0:60], w2s[:, kt * P:(kt + 1) * P], hcT[:, kt * 64:kt * 64 + 60],
                                 start=kt == 0, stop=kt == 1)
            for gq in range(KVG):
                for kt in range(2):
                    at = (2 + kt) * 64 + gq * CB
                    m = nc.tensor.matmul(SIDE[1][0:CB, COLS + gq * P:COLS + (gq + 1) * P], hcT[:, at:at + CB],
                                         w2s[:, 256 + kt * P:256 + (kt + 1) * P], start=kt == 0, stop=kt == 1)
            m.then_inc(side_full[1], 1)

        def att_step_tensor(pe, name, p, g, it):
            wait_past(pe, side_out[p], ATTN.before(name, it))
            dst = SIDE[p]
            b = "ab".find(name[-1])
            if name == "gates":
                tail_tensor(pe, 1, ATTN.before(name, it), 48)
            elif name[:3] == "sc1":
                if b == 0:
                    pe.wait_ge(side_out[1], ATTN.before("sc0a", it))
                for hl in range(4):
                    m = nc.tensor.matmul(dst[:, hl * SEQ:(hl + 1) * SEQ], qT[:, hl * SEQ + P:(hl + 1) * SEQ],
                                         kT[b][:, ds(g * SEQ, SEQ)], **ONE)
                m.then_inc(side_full[p], 1)
            elif name[:3] == "sc0":
                for hl in range(4):
                    m = nc.tensor.matmul(dst[:, hl * P:(hl + 1) * P], qT[:, hl * SEQ:hl * SEQ + P],
                                         kT[b][:, ds(g * SEQ, P)], **ONE)
                m.then_inc(side_full[p], 1)
            elif name[:3] == "pt1":
                pe.wait_ge(p_exp, g * 4 + 2 * b + 1)
                turn([(i * P, sm1[:, i * P:(i + 1) * P]) for i in range(8)], p)
            elif name[:3] == "pt0":
                pe.wait_ge(p_exp, g * 4 + 2 * b + 2)
                turn([(i * P, sm0[:, i * P:(i + 1) * P]) for i in range(4)], p)
            elif name[:2] == "pv" and b >= 0:
                pe.wait_ge(side_out[0], ATTN.after(f"pt1{name[-1]}", it))
                pe.wait_ge(side_out[1], ATTN.after(f"pt0{name[-1]}", it))
                for hl in range(4):
                    nc.tensor.matmul(dst[:, hl * P:(hl + 1) * P], p0T[:, hl * P:(hl + 1) * P],
                                     vS[b][:, ds(g * P, P)], **ONE)
                    for kt in range(2):
                        m = nc.tensor.matmul(dst[:, (4 + hl) * P:(5 + hl) * P],
                                             p1T[:, (hl * 2 + kt) * P:(hl * 2 + kt + 1) * P],
                                             vS[b][:, ds(g * P + kt * COLS, P)], start=kt == 0, stop=kt == 1)
                m.then_inc(side_full[p], 1)
            elif name == "scc":
                for u in range(8):
                    at = (u % 4) * SEQ + (u // 4) * P
                    m = nc.tensor.matmul(dst[:, u * CB:(u + 1) * CB], qT[:, at:at + P], kcT[:, ds(g * CB, CB)], **ONE)
                m.then_inc(side_full[p], 1)
            elif name == "ptc":
                pe.wait_ge(pc_ready, g + 1)
                for u in range(8):
                    m = nc.tensor.transpose(dst[0:CB, u * P:(u + 1) * P], scc[:, u * CB:(u + 1) * CB], ident)
                m.then_inc(side_full[p], 1)
            elif name == "pvc":
                pe.wait_ge(side_out[0], ATTN.after("ptc", it))
                for u in range(8):
                    m = nc.tensor.matmul(dst[:, u * P:(u + 1) * P], pcT[:, u * P:(u + 1) * P],
                                         vc[:, ds(g * P, P)], **ONE)
                m.then_inc(side_full[p], 1)
            elif name == "o_t":
                pe.wait_ge(att_done, g + 1)
                turn(by_unit(oacc), p)
            elif name == "q_t":
                pe.wait_ge(acc_out[0], ATTN.after("q", it))
                turn(by_block(qtok), p)

        def att_tensor(pe, it):
            c, which = att_c(it), att_which(it)
            for hs in range(16):
                j, half = hs // 2, hs % 2
                if j < 4 and PROJ in which:
                    if hs == 0:
                        pe.wait_ge(acc_out[0], ATTN.before("q", it))
                    if half == 0 and ONCE in which:
                        pe.wait_ge(side_out[j % 2], NORM3.after(f"norm{j}", 0))
                    products(pe, c, hs, 0, X_HI, X_LO, j == 0, j == 3, 4 * j)
                if j >= 4 and OUT in which:
                    acc = (j + 1) % 2
                    if half == 0:
                        pe.wait_ge(acc_out[acc], ATTN.before(f"out{j - 4}", it))
                        if j == 4:
                            pe.wait_ge(side_out[0], ATTN.before("sc1a", it) if ATT in which else ATTN.end["x0"])
                    products(pe, c, hs, acc, A_HI, A_LO, True, True)
                    if half and j > 4 and ATT not in which:
                        norm_tensor(pe, NORM4, j - 5, (j % 2, ATTN.after(f"out{j - 5}", it)))
                for name, p, w_ in steps_at(ATT_STEPS, hs, which):
                    att_step_tensor(pe, name, p, it - 1 if w_ == ATT else it, it)
            if ATT not in which and OUT in which:
                norm_tensor(pe, NORM4, 3, (0, ATTN.after("out3", it)))

        def split_hi(act, c, h):
            if isinstance(c, int) and c + h >= 2 * CHUNKS:
                return
            act.wait_ge(raw_full[h // 2 % RAWS], c * 2 + 16 * (h // (2 * RAWS) + 1))
            if not (isinstance(c, int) and c + h < WS):
                act.wait_ge(w_used, c + (h + 1 - WS))
            nc.scalar.activation(W_HI[:, h % WS, :], raw_piece(h), ACT.Copy).then_inc(hi_ready, 1)

        def take_out(act, p, n, dst, src=None, func=ACT.Copy, **more):
            act.wait_ge(side_full[p], n)
            nc.scalar.activation(dst, SIDE[p][:, :] if src is None else src, func, **more).then_inc(side_out[p], 1)

        def stripe_out(acc, dst, scale, func=ACT.Copy):
            for t in range(NT):
                i = nc.scalar.activation(dst[:, t * COLS:(t + 1) * COLS], ACC[acc][:, t * COLS:(t + 1) * COLS], func,
                                         scale=scale[:, t:t + 1])
            i.then_inc(acc_out[acc], 1)

        def norm_scalar(act, norm, nth, r, gain):
            act.wait_ge(side_full[r % 2], norm.after(f"norm{r}", 0))
            for q in range(4):
                kt = 4 * r + q
                i = nc.scalar.activation(X_HI[:, kt * SEQ:(kt + 1) * SEQ], SIDE[r % 2][:, q * SEQ:(q + 1) * SEQ],
                                         ACT.Copy, scale=PRM[:, A_GAIN + gain * KT + kt:A_GAIN + gain * KT + kt + 1])
            i.then_inc(x_hi, 1)

        def squares(act, nth, ready, to):
            for p in range(2):
                if ready:
                    act.wait_ge(acc_out[p], ready[f"a{p}"])
            for t in range(NT):
                if t:
                    act.wait_ge(sumsq, 2 * nth + 1)
                nc.scalar.activation(to[t], H[:, t, :], ACT.Square, accum_out=sumsq_c[:, t:t + 1]).then_inc(sumsq, 1)

        def act_in_scalar(act, p, n, used):
            act.wait_ge(w_used, used)
            act.wait_ge(side_full[p], n)
            nc.scalar.activation(A_HI[:, :], SIDE[p][:, :], ACT.Copy).then_inc(act_hi, 1)

        def tail_scalar(act, nth, raw):
            act.wait_ge(tail_in, 16 * nth + 16)
            nc.scalar.activation(A_HI[:, 0:raw.shape[1]], raw, ACT.Copy).then_inc(tail_hi, 1)

        def gdn_step_scalar(act, name, p, g, it, used):
            n = GDN.after(name, it) if p is not None else None
            kind = name[0] if name[1:].isdigit() else name
            if name == "gates1":
                act.wait_ge(gate_abs, 1)
                nc.scalar.activation(bet, bav[:, :, 0:32], ACT.Exp, scale=-1.0).then_inc(gate_exp, 1)
                nc.scalar.activation(eal, PRM[:, A_ALOG:A_ALOG + HEADS], ACT.Exp).then_inc(gate_ea, 1)
                nc.scalar.activation(spl, spl, ACT.Exp, scale=-1.0).then_inc(gate_exp, 1)
                act.wait_ge(gate_exp, 2)
                nc.scalar.activation(spl, spl, ACT.Ln, bias=1.0).then_inc(gate_ln, 1)
            elif name == "gates2":
                act.wait_ge(gate_cum, 1)
                nc.scalar.activation(egc, gcl[:, 32:64], ACT.Exp).then_inc(gate_fac, 1)
                nc.scalar.activation(kdx, kdx, ACT.Exp).then_inc(gate_fac, 1)
            elif name in ("qk_t", "v_t"):
                wait_past(act, conv_done, g * 4 + (2 if name == "v_t" else 0))
                take_out(act, p, n, cin[:, :, 3:3 + SEQ], SIDE[p][:, :].rearrange("p (b n) -> p b n", n=SEQ))
            elif name == "silu_qk":
                act.wait_ge(conv_done, g * 4 + 2)
                nc.scalar.activation(cq, cq, ACT.Silu).then_inc(silu_done, 1)
            elif name == "squares":
                act.wait_ge(silu_done, g * 2 + 1)
                if not isinstance(it, int):
                    act.wait_ge(side_full[1], GDN.after("o_t", it))
                nc.scalar.activation(ES, cq, ACT.Square).then_inc(sq_done, 1)
            elif name == "silu_v":
                act.wait_ge(conv_done, g * 4 + 4)
                nc.scalar.activation(cv, cv, ACT.Silu).then_inc(silu_done, 1)
            elif name == "ss":
                take_out(act, p, n, ES, func=ACT.Ln, bias=eps_col)
                act.wait_ge(side_out[p], n)
                nc.scalar.activation(ES, ES, ACT.Exp, scale=-0.5).then_inc(rb_done, 1)
            elif name == "gb":
                act.wait_ge(dif_done, g + 1)
                nc.scalar.activation(E, E, ACT.Exp).then_inc(exp_done, 1)
            elif name == "lt":
                take_out(act, p, n, N)
            elif name == "at":
                take_out(act, p, n, AT)
            elif kind == "y":
                take_out(act, p, n, YR[:, :])
            elif name == "v0":
                take_out(act, p, n, E[:, 0:512], SIDE[p][:, 0:512])
            elif name == "s":
                take_out(act, p, n, S, SIDE[p][:, 0:512])
            elif name == "v1":
                take_out(act, p, n, E[:, 512:1024], SIDE[p][:, 0:512])
            elif name == "osum":
                act.wait_ge(side_out[0], GDN.after("o", it))
                nc.scalar.activation(N, ES, ACT.Square).then_inc(osq_done, 1)
            elif name == "o_t":
                act_in_scalar(act, p, n, used)

        def gdn_scalar(act, it):
            which = gdn_which(it)
            for hs in range(32):
                j, c = hs // 2, gdn_c(it, hs)
                if hs % 2 and j % 4 == 3 and j // 4 != 1 and PREP in which:
                    part = GDN_PART[j // 4]
                    act.wait_ge(w_used, c + (hs + 1))
                    if ONCE in which:
                        act.wait_ge(rstd, 1)
                    if part == "z":
                        wait_past(act, o_scaled, it)
                        stripe_out(GDN_ACC[part], zs, rstd_c, ACT.Silu)
                    else:
                        stripe_out(GDN_ACC[part], tokraw, rstd_c)
                if hs % 2 and 4 < j < 8 and which == (OUT,):
                    norm_scalar(act, NORM1, 1, j - 5, 1)
                for name, p, w_ in steps_at(GDN_STEPS, hs, which):
                    gdn_step_scalar(act, name, p, it - 1 if w_ == SOLVE else it, it, c + 16)
                if gdn_section(j, which):
                    split_hi(act, c, hs + WS)
            if which == (OUT,):
                norm_scalar(act, NORM1, 1, 3, 1)
                squares(act, 1, GDN.end, [junk, junk])

        def ffn_scalar(act, ph, base, it, nrm, nxt):
            c = ffn_c(base, it)
            first, final_ = (isinstance(it, int) and it == n for n in (0, FBLK))
            for k in range(12):
                if (k < 8 and final_) or (k >= 8 and first):
                    continue
                for half in range(2):
                    split_hi(act, c, 2 * k + half + WS)
                if k == 3:
                    act.wait_ge(w_used, c + 8)
                    act.wait_ge(acc_out[1], ph.before("up", it))
                    if first:
                        act.wait_ge(rstd, nrm)
                    stripe_out(0, sg, rstd_c, ACT.Silu)
                if k > 8 and final_ and nxt:
                    norm_scalar(act, nxt[0], nxt[1], k - 9, nxt[2])
            if not final_:
                act_in_scalar(act, 0, ph.after("hid_t", it), c + (16 if first else 24))
            elif nxt:
                norm_scalar(act, nxt[0], nxt[1], 3, nxt[2])
                squares(act, 2, ph.end, [junk, junk])

        def kv_scalar(act):
            act.wait_ge(rstd, 3)
            for s in range(6):
                acc = s % 2
                for k in range(8):
                    split_hi(act, 2 * B_KV, 8 * s + k + WS)
                    if s == 5 and k == 4:
                        blocks_hi(act, 0)
                    if k == 2 and s - 1 in KV_TURNED:
                        take_out(act, 1 - acc, KV.after(f"kv_t{s - 1}", 0), KV_TO[s - 1])
                act.wait_ge(w_used, 2 * B_KV + 8 * s + 8)
                stripe_out(acc, vS[(s - 3) // 2] if s in (3, 5) else tkv[acc], rstd_c)

        def blocks_hi(act, kv):
            act.wait_ge(w_used, 2 * B_CMP - (0 if kv else 4))
            act.wait_ge(xp_done, kv + 1)
            nc.scalar.activation(X_HI[:, kv * 2048:kv * 2048 + 1920], XP[:, 0:1920], ACT.Copy).then_inc(xp_hi, 1)

        def compress_scalar(act):
            blocks_hi(act, 1)
            for kv in range(2):
                for k in range(8):
                    split_hi(act, 2 * B_CMP, 8 * kv + k + WS)
                act.wait_ge(w_used, 2 * B_CMP + 8 * kv + 8)
                nc.scalar.activation(hc[0:60, kv * 256:(kv + 1) * 256], ACC[kv][0:60, 0:256], ACT.Silu)\
                  .then_inc(acc_out[kv], 1)
            def rows(ap):
                return ap.rearrange("p (i n) -> p i n", n=64)[:, :, 0:60]
            take_out(act, 0, CMP.after("hid_t", 0), rows(hcT), rows(SIDE[0][:, 0:256]))
            act.wait_ge(side_full[1], CMP.after("w2", 0))
            nc.scalar.activation(kcT[:, 0:60], SIDE[1][:, 0:60], ACT.Copy)
            nc.scalar.activation(vc, SIDE[1][0:CB, COLS:2 * COLS], ACT.Copy).then_inc(side_out[1], 1)

        def att_step_scalar(act, name, p, g, it, used):
            n = ATTN.after(name, it)
            b = "ab".find(name[-1])
            if name == "gates":
                act.wait_ge(side_full[0], n)
                for t in range(NT):
                    i = nc.scalar.activation(gsig[:, t * 48:(t + 1) * 48], SIDE[0][:, t * COLS:t * COLS + 48], ACT.Exp,
                                             scale=SM[:, 6 + t:7 + t])
                i.then_inc(side_out[0], 1)
            elif name[:2] == "sc" and b >= 0:
                t = int(name[2])
                sm, wd = (sm1, SEQ) if t else (sm0, P)
                act.wait_ge(mx_done, g * 4 + (2 * b + 2 - t))
                for hl in range(4):
                    part = sm[:, hl * wd:(hl + 1) * wd]
                    at = b * 8 + t * 4 + hl
                    i = nc.scalar.activation(part, part, ACT.Exp, bias=mxs[:, t * 4 + hl:t * 4 + hl + 1],
                                             accum_out=sums[:, at:at + 1])
                i.then_inc(p_exp, 1)
            elif name[:3] == "pt1":
                take_out(act, p, n, p1T)
            elif name[:3] == "pt0":
                take_out(act, p, n, p0T, SIDE[1][:, 0:512])
            elif name == "scc":
                act.wait_ge(sc_max, g + 1)
                nc.scalar.activation(scc, scc, ACT.Exp).then_inc(sc_exp, 1)
            elif name == "ptc":
                take_out(act, p, n, pcT, SIDE[0][0:CB, :])
            elif name == "o_t":
                act_in_scalar(act, p, n, used)
            elif name == "q_t":
                take_out(act, p, n, qT)

        def att_scalar(act, it):
            c, which = att_c(it), att_which(it)
            for hs in range(16):
                j = hs // 2
                if hs % 2 and (PROJ if j < 4 else OUT) in which:
                    if j == 3:
                        act.wait_ge(w_used, c + 8)
                        stripe_out(0, qtok, rstd_q)
                    if j > 4 and ATT not in which:
                        norm_scalar(act, NORM4, 4, j - 5, 4)
                for name, p, w_ in steps_at(ATT_STEPS, hs, which):
                    att_step_scalar(act, name, p, it - 1 if w_ == ATT else it, it, c + (16 if OUT in which else 8))
                if (PROJ if j < 4 else OUT) in which:
                    split_hi(act, c, hs + WS)
            if ATT not in which and OUT in which:
                norm_scalar(act, NORM4, 4, 3, 4)
                squares(act, 3, ATTN.end, [junk, junk])

        def split_lo(dve, c, h):
            if isinstance(c, int) and c + h >= 2 * CHUNKS:
                return
            dve.wait_ge(hi_ready, c + (h + 1))
            nc.vector.tensor_tensor(W_LO[:, h % WS, :], raw_piece(h), W_HI[:, h % WS, :].bitcast(f32),
                                    SUB).then_inc(lo_ready, 1)

        def norm_vector(dve, norm, nth, r, gain):
            dve.wait_ge(x_hi, 4 * nth + r + 1)
            for q in range(4):
                kt = 4 * r + q
                at = slice(kt * SEQ, (kt + 1) * SEQ)
                i = nc.vector.scalar_tensor_tensor(X_LO[:, at], SIDE[r % 2][:, q * SEQ:(q + 1) * SEQ],
                                                   PRM[:, A_GAIN + gain * KT + kt:A_GAIN + gain * KT + kt + 1],
                                                   X_HI[:, at].bitcast(f32), MUL, SUB)
            i.then_inc(side_out[r % 2], 1)

        def add_to_h(dve, c, k, acc, stripe):
            dve.wait_ge(w_used, c + 2 * (k + 1))
            dst = H[:, :, stripe * COLS:(stripe + 1) * COLS]
            nc.vector.tensor_tensor(dst, dst, tiles2(ACC[acc][:, :]), ADD).then_inc(acc_out[acc], 1)

        def act_in_vector(dve, p, nth):
            dve.wait_ge(act_hi, nth)
            nc.vector.tensor_tensor(A_LO[:, :], SIDE[p][:, :], A_HI[:, :].bitcast(f32), SUB).then_inc(side_out[p], 1)

        def tail_vector(dve, nth, raw):
            dve.wait_ge(tail_hi, nth + 1)
            n = raw.shape[1]
            nc.vector.tensor_tensor(A_LO[:, 0:n], raw, A_HI[:, 0:n].bitcast(f32), SUB).then_inc(tail_lo, 1)

        ba = w(12 * 1024, 512)
        bav, bet, spl, gg = (tiles2(ba[:, a:b]) for a, b in ((0, 128), (128, 192), (192, 256), (256, 320)))
        gcl, eal, kdx, egc = ba[:, 320:416], ba[:, 416:448], ba[:, 448:480], ba[:, 480:512]
        GAg = GA[:, :].rearrange("p (g c) -> p g c", c=GW)

        def heads(ap):
            return ap.rearrange("p (g h) -> p g h", h=4)

        def conv(link, dst, nth, blocks):
            for tap in range(4):
                for b in blocks:
                    wc = CW[:, 16 * nth + 4 * b + tap:16 * nth + 4 * b + tap + 1]
                    d, src = dst[:, b * SEQ:(b + 1) * SEQ], cin[:, b, tap:tap + SEQ]
                    if tap == 0:
                        i = nc.vector.tensor_scalar(d, src, wc, None, MUL)
                    else:
                        i = nc.vector.scalar_tensor_tensor(d, src, wc, d, MUL, ADD)
                if tap < 3:
                    link(i)
            i.then_inc(conv_done, 1)

        def gates1_vector(dve, link, n):
            dve.wait_ge(side_full[0], n)
            dve.wait_ge(rstd, 1)
            for t in range(NT):
                i = nc.vector.tensor_scalar(bav[:, t, 0:64], SIDE[0][:, t * COLS:t * COLS + 64], rstd_c[:, t:t + 1],
                                            None, MUL)
            i.then_inc(side_out[0], 1)
            dve.wait_ge(side_out[0], n)
            dt_b = PRM[:, A_DT:A_DT + HEADS].unsqueeze(1).broadcast_to([P, NT, HEADS])
            link(nc.vector.tensor_tensor(gg, bav[:, :, 32:64], dt_b, ADD))
            nc.vector.scalar_tensor_tensor(spl, gg, -1.0, gg, MUL, ALU.max).then_inc(gate_abs, 1)
            dve.wait_ge(gate_exp, 2)
            link(nc.vector.tensor_scalar(bet, bet, 1.0, None, ADD))
            link(nc.vector.reciprocal(bet, bet))
            dve.wait_ge(gate_ln, 1)
            link(nc.vector.scalar_tensor_tensor(gg, gg, 0.0, spl, ALU.max, ADD))
            dve.wait_ge(gate_ea, 1)
            nc.vector.scalar_tensor_tensor(gg, gg, -1.0, eal.unsqueeze(1).broadcast_to([P, NT, HEADS]), MUL, MUL)\
              .then_inc(gate_g, 1)

        def gates2_vector(dve, link, n):
            dve.wait_ge(side_full[0], n)
            nc.vector.tensor_copy(gcl, SIDE[0][:, 0:96]).then_inc(side_out[0], 1)
            dve.wait_ge(side_out[0], n)
            nc.vector.tensor_tensor(kdx, gcl[:, 64:96], gcl[:, 0:32], SUB).then_inc(gate_cum, 1)
            dve.wait_ge(gate_g, 1)
            for t in range(NT):
                nc.vector.tensor_copy(GAg[:, :, 4 * t:4 * t + 4], heads(bet[:, t, :]))
                nc.vector.tensor_copy(GAg[:, :, 8 + 4 * t:12 + 4 * t], heads(gg[:, t, :]))
                nc.vector.tensor_copy(GAg[:, :, 16 + 4 * t:20 + 4 * t], heads(gcl[:, 32 * t:32 * t + 32]))
            dve.wait_ge(gate_fac, 2)
            nc.vector.tensor_copy(GAg[:, :, 28:32], heads(egc))
            nc.vector.tensor_copy(GAg[:, :, 32:36], heads(kdx))
            link(nc.vector.scalar_tensor_tensor(GAg[:, :, 24:28], heads(bet[:, 1, :]), -1.0, heads(egc), MUL, MUL))

        def gdn_step_vector(dve, link, name, p, g, it):
            n = GDN.after(name, it) if p is not None else None
            kind = name[0] if name[1:].isdigit() else name
            side = SIDE[p] if p is not None else None
            if name == "gates1":
                gates1_vector(dve, link, n)
            elif name == "gates2":
                gates2_vector(dve, link, n)
            elif name == "conv_qk0":
                link(nc.vector.tensor_copy(CW[:, :], PRM[:, ds(g * 32 + A_CONV, 32)]))
                dve.wait_ge(side_out[1], GDN.after("qk_t", it))
                conv(link, cq, 0, (0, 1))
            elif name == "conv_qk1":
                conv(link, cq, 0, (2, 3))
            elif name == "conv_v0":
                dve.wait_ge(side_out[1], GDN.after("v_t", it))
                conv(link, cv, 1, (0, 1))
            elif name == "conv_v1":
                conv(link, cv, 1, (2, 3))
            elif name == "ss":
                dve.wait_ge(rb_done, g + 1)
                nc.vector.scalar_tensor_tensor(qkn[:, 0:512], cq[:, 0:512], D_SC, ES[:, 0:512], MUL, MUL)
                nc.vector.tensor_tensor(qkn[:, 512:1024], cq[:, 512:1024], ES[:, 512:1024], MUL).then_inc(qkn_done, 1)
            elif name == "factors":
                nc.vector.tensor_copy(GP[:, :], GA[:, ds(g * GW, GW)]).then_inc(gp_ready, 1)
            elif name == "k_t":
                dve.wait_ge(side_full[p], n)
                dve.wait_ge(gp_ready, g + 1)
                for hl in range(4):
                    i = nc.vector.tensor_scalar(kd[:, hl * P:(hl + 1) * P], side[:, (hl // 2) * P:(hl // 2 + 1) * P],
                                                GP[:, 32 + hl:33 + hl], None, MUL)
                i.then_inc(side_out[p], 1)
            elif name == "gb":
                dve.wait_ge(side_full[p], n)
                nc.vector.tensor_tensor(units(E), each(GP[:, 16:24]), units(side[:, :]), SUB).then_inc(side_out[p], 1)
                dve.wait_ge(side_out[p], n)
                nc.vector.tensor_scalar(E, E, 0.0, None, ALU.min).then_inc(dif_done, 1)
            elif name == "kkqk":
                dve.wait_ge(decay_ready, g + 1)
                dve.wait_ge(side_full[p], n)
                for of, buf in ((0, ES), (1, E)):
                    src = units(side[:, of * 512:(of + 1) * 512]).unsqueeze(2).broadcast_to([P, 4, 2, P])
                    b4 = buf.rearrange("p (a b n) -> p a b n", b=2, n=P)
                    i = nc.vector.tensor_tensor(b4, src, b4, MUL)
                i.then_inc(side_out[p], 1)
            elif name == "v_t2":
                dve.wait_ge(side_full[p], n)
                nc.vector.tensor_tensor(units(vb), units(side[:, :]), each(GP[:, 0:8]), MUL).then_inc(side_out[p], 1)
            elif kind in ("t", "u"):
                buf = TR if kind == "t" else UR
                dve.wait_ge(side_full[p], n)
                nc.vector.tensor_tensor(buf[:, :], buf[:, :].bitcast(f32), side[:, :], SUB).then_inc(side_out[p], 1)
            elif name == "nw":
                dve.wait_ge(side_full[p], n)
                link(nc.vector.scalar_tensor_tensor(UF, TR[:, :].bitcast(f32), -1.0, side[:, :], MUL, SUB))
                nc.vector.tensor_tensor(units(YR[:, :]), units(UF), every(K_ID), ADD).then_inc(side_out[p], 1)
            elif name == "ru":
                dve.wait_ge(side_full[p], n)
                nc.vector.tensor_tensor(UF, UR[:, :].bitcast(f32), side[:, :], ADD).then_inc(side_out[p], 1)
            elif name == "ks":
                dve.wait_ge(side_full[p], n)
                nc.vector.tensor_tensor(units(vb[:, 0:512]), units(side[:, 512:1024]), each(GP[:, 28:32], 4), MUL)
                for hl in range(4):
                    part = vb[:, 512 + hl * P:512 + (hl + 1) * P]
                    i = nc.vector.scalar_tensor_tensor(part, side[:, hl * P:(hl + 1) * P], GP[:, 24 + hl:25 + hl], part,
                                                       MUL, ADD)
                i.then_inc(side_out[p], 1)
            elif name == "o":
                dve.wait_ge(side_full[p], n)
                nc.vector.tensor_copy(ES[:, 0:512], side[:, 0:512])
                nc.vector.tensor_tensor(ES[:, 512:1024], side[:, 512:1024], vb[:, 0:512], ADD).then_inc(side_out[p], 1)
            elif name == "osum":
                dve.wait_ge(osq_done, g + 1)
                link(nc.vector.reduce_sum(osum_c, units(N), axis=AX.X))
                nc.vector.tensor_scalar(osum_c, osum_c, 1.0 / P, EPS, MUL, ADD).then_inc(osum_done, 1)
            elif name == "oscale":
                dve.wait_ge(ors_done, g + 1)
                link(nc.vector.tensor_tensor(units(ES), units(ES), each(ors_c), MUL))
                dve.wait_ge(zg_ready, g + 1)
                nc.vector.tensor_tensor(ES, ES, zs, MUL).then_inc(o_scaled, 1)
            elif name == "o_t":
                act_in_vector(dve, p, g + 1)

        def gdn_vector(dve, link, it):
            which = gdn_which(it)
            for hs in range(32):
                j, c = hs // 2, gdn_c(it, hs)
                if hs % 2 and j // 4 == 1 and OUT in which:
                    add_to_h(dve, c, j, (j + 1) % 2, j - 4)
                    if j > 4 and which == (OUT,):
                        norm_vector(dve, NORM1, 1, j - 5, 1)
                for name, p, w_ in steps_at(GDN_STEPS, hs, which):
                    gdn_step_vector(dve, link, name, p, it - 1 if w_ == SOLVE else it, it)
                if gdn_section(j, which):
                    split_lo(dve, c, hs + WS)
            if which == (OUT,):
                norm_vector(dve, NORM1, 1, 3, 1)

        def ffn_vector(dve, ph, base, it, hi0, nxt):
            c = ffn_c(base, it)
            first, final_ = (isinstance(it, int) and it == n for n in (0, FBLK))
            for k in range(12):
                if (k < 8 and final_) or (k >= 8 and first):
                    continue
                if k == 7:
                    dve.wait_ge(acc_out[0], ph.after("gate", it))
                    dve.wait_ge(w_used, c + 16)
                    for t in range(NT):
                        at = slice(t * COLS, (t + 1) * COLS)
                        i = nc.vector.scalar_tensor_tensor(hid[:, at], ACC[1][:, at], rstd_c[:, t:t + 1], sg[:, at],
                                                           MUL, MUL)
                    i.then_inc(acc_out[1], 1)
                if k >= 8:
                    add_to_h(dve, c, k, k % 2, k - 8)
                for half in range(2):
                    split_lo(dve, c, 2 * k + half + WS)
                if k > 8 and final_ and nxt:
                    norm_vector(dve, nxt[0], nxt[1], k - 9, nxt[2])
            if not final_:
                act_in_vector(dve, 0, it + (hi0 + 1))
            elif nxt:
                norm_vector(dve, nxt[0], nxt[1], 3, nxt[2])

        def blocks_vector(dve, kv):
            src = kvT[kv].rearrange("p (g n r) -> p g n r", g=KVG, r=16)
            dst = XP[:, 0:CMPB * 60].rearrange("p (h r g n) -> p h r g n", h=2, g=KVG, n=CB)
            for half in range(2):
                for gq in range(KVG):
                    tok = src[:, gq, half:half + CB, :].rearrange("p n r -> p r n")
                    pos = PRM[:, A_POS + 16 * half:A_POS + 16 * half + 16]
                    i = nc.vector.tensor_tensor(dst[:, half, :, gq, :], tok, each(pos, 16, CB), ADD)
            i.then_inc(xp_done, 1)

        def kv_vector(dve):
            for h in range(2 * C_KV):
                split_lo(dve, 2 * B_KV, h + WS)
                if h == 32:
                    dve.wait_ge(side_out[0], KV.after("kv_t0", 0))
                    blocks_vector(dve, 0)
                if h == 2 * C_KV - 2:
                    blocks_rest(dve, 0)

        def blocks_rest(dve, kv):
            dve.wait_ge(xp_hi, kv + 1)
            at = slice(kv * 2048, kv * 2048 + 1920)
            nc.vector.tensor_tensor(X_LO[:, at], XP[:, 0:1920], X_HI[:, at].bitcast(f32), SUB).then_inc(xp_lo, 1)

        def compress_vector(dve):
            dve.wait_ge(xp_lo, 1)
            dve.wait_ge(side_out[1], KV.after("kv_t1", 0))
            blocks_vector(dve, 1)
            blocks_rest(dve, 1)
            for h in range(2 * C_CMP):
                split_lo(dve, 2 * B_CMP, h + WS)

        slp, gcol = GP[:, 24:28], GP[:, 0:24]
        sums, mxs, coef, cmx = small[:, 0:24], small[:, 24:32], small[:, 32:40], small[:, 40:48]

        def weigh(dve, link, p, n, b, dst):
            link(nc.vector.reciprocal(coef, sums[:, b[0] * 8:b[0] * 8 + 8]))
            link(nc.vector.tensor_tensor(coef, coef, gcol[:, b[1] * 8:b[1] * 8 + 8], MUL))
            dve.wait_ge(side_full[p], n)
            nc.vector.tensor_tensor(units(dst), units(SIDE[p][:, :]), each(coef), MUL).then_inc(side_out[p], 1)
            dve.wait_ge(side_out[p], n)

        def att_step_vector(dve, link, name, p, g, it):
            n = ATTN.after(name, it)
            b = "ab".find(name[-1])
            if name == "gates":
                dve.wait_ge(side_out[0], n)
                link(nc.vector.tensor_scalar(gsig, gsig, 1.0, None, ADD))
                link(nc.vector.reciprocal(gsig, gsig))
                gv = GA[:, 0:KVG * AW].rearrange("p (g c) -> p g c", c=AW)
                for t in range(NT):
                    for br in range(3):
                        src = gsig[:, t * 48 + br * 16:t * 48 + br * 16 + 16].rearrange("p (g h) -> p g h", h=4)
                        nc.vector.tensor_copy(gv[:, :, br * 8 + t * 4:br * 8 + t * 4 + 4], src)
                link(nc.vector.tensor_copy(gv[:, :, 24:28], K[:, K_SL:K_SL + 16].rearrange("p (g h) -> p g h", h=4)))
            elif name[:2] == "sc" and b >= 0:
                if name == "sc1a":
                    link(nc.vector.tensor_copy(GP[:, 0:AW], GA[:, ds(g * AW, AW)]))
                t = int(name[2])
                sm, wd, dist = (sm1, SEQ, K_D1) if t else (sm0, P, K_D0)
                dve.wait_ge(side_full[p], n)
                for hl in range(4):
                    at = slice(hl * wd, (hl + 1) * wd)
                    i = nc.vector.scalar_tensor_tensor(sm[:, at], K[:, dist:dist + wd], slp[:, hl:hl + 1],
                                                       SIDE[p][:, at], MUL, ADD)
                i.then_inc(side_out[p], 1)
                dve.wait_ge(side_out[p], n)
                mx = mxs[:, 4 * t:4 * t + 4]
                link(nc.vector.reduce_max(mx, units(sm, wd), axis=AX.X))
                nc.vector.tensor_scalar(mx, mx, -1.0, None, MUL).then_inc(mx_done, 1)
            elif name[:2] == "pv" and b >= 0:
                dve.wait_ge(p_exp, g * 4 + 2 * b + 2)
                weigh(dve, link, p, n, (b, b + 1), tmpo if b else oacc)
                if b:
                    link(nc.vector.tensor_tensor(oacc, oacc, tmpo, ADD))
            elif name == "scc":
                for t in range(NT):
                    cd = K[:, K_CD + t * CB:K_CD + (t + 1) * CB].unsqueeze(1).broadcast_to([P, 4, CB])
                    i = nc.vector.tensor_tensor(units(scb, CB)[:, 4 * t:4 * t + 4, :], cd, each(slp, 4, CB), MUL)
                link(i)
                dve.wait_ge(side_full[p], n)
                nc.vector.tensor_tensor(scc, scb, SIDE[p][:, 0:8 * CB], ADD).then_inc(side_out[p], 1)
                dve.wait_ge(side_out[p], n)
                link(nc.vector.reduce_max(cmx, units(scc, CB), axis=AX.X))
                nc.vector.tensor_tensor(units(scc, CB), units(scc, CB), each(cmx, 8, CB), SUB).then_inc(sc_max, 1)
                dve.wait_ge(sc_exp, g + 1)
                link(nc.vector.reduce_sum(sums[:, 16:24], units(scc, CB), axis=AX.X))
                for t in range(NT):
                    seen = K[:, K_CV + t * CB:K_CV + (t + 1) * CB].unsqueeze(1).broadcast_to([P, 4, CB])
                    part = units(scc, CB)[:, 4 * t:4 * t + 4, :]
                    i = nc.vector.tensor_tensor(part, part, seen, MUL)
                i.then_inc(pc_ready, 1)
            elif name == "pvc":
                weigh(dve, link, p, n, (2, 0), tmpo)
                nc.vector.tensor_tensor(oacc, oacc, tmpo, ADD).then_inc(att_done, 1)
            elif name == "o_t":
                act_in_vector(dve, p, g + (GROUPS + FBLK + 1))

        def att_vector(dve, link, it):
            c, which = att_c(it), att_which(it)
            for hs in range(16):
                j = hs // 2
                if hs % 2 and (PROJ if j < 4 else OUT) in which:
                    if j >= 4:
                        add_to_h(dve, c, j, (j + 1) % 2, j - 4)
                    if j > 4 and ATT not in which:
                        norm_vector(dve, NORM4, 4, j - 5, 4)
                for name, p, w_ in steps_at(ATT_STEPS, hs, which):
                    att_step_vector(dve, link, name, p, it - 1 if w_ == ATT else it, it)
                if (PROJ if j < 4 else OUT) in which:
                    split_lo(dve, c, hs + WS)
            if ATT not in which and OUT in which:
                norm_vector(dve, NORM4, 4, 3, 4)

        def rstd_pool(pool, link, nth):
            pool.wait_ge(sumsq, 2 * nth + 2)
            link(nc.gpsimd.tensor_scalar(rstd_c, sumsq_c, 1.0 / DM, EPS, MUL, ADD))
            link(nc.gpsimd.tensor_tensor(rstd_c, rstd_c, minus_half[:, 0:2], ALU.pow))
            nc.gpsimd.tensor_scalar(SM[:, 6:8], rstd_c, -1.0, None, MUL)
            nc.gpsimd.tensor_scalar(rstd_q, rstd_c, D_SC, None, MUL).then_inc(rstd, 1)

        def gdn_step_pool(pool, link, name, p, g, it):
            kind, lv = name[0], int(name[1:]) if name[1:].isdigit() else None

            def mask(level):
                nc.gpsimd.tensor_tensor(units(NS[level % 2][:, :]), units(N), every(K_LV + level * P), MUL)\
                  .then_inc(ns_ready, 1)

            if name == "factors":
                pool.wait_ge(gp_ready, g + 1)
                nc.gpsimd.tensor_tensor(units(E), each(GP[:, 8:16]), every(K_ONE), MUL).then_inc(gbc_done, 1)
            elif name == "gb":
                pool.wait_ge(exp_done, g + 1)
                link(nc.gpsimd.tensor_tensor(units(E), units(E), every(K_LOW), MUL))
            elif name == "ss":
                pool.wait_ge(qkn_done, g + 1)
                link(nc.gpsimd.tensor_tensor(units(ES), each(GP[:, 0:8]), every(K_STR), MUL))
                nc.gpsimd.tensor_tensor(ES, ES, E, MUL).then_inc(decay_ready, 1)
            elif name == "kkqk":
                pool.wait_ge(side_out[1], GDN.after(name, it))
                link(nc.gpsimd.tensor_tensor(units(TR[:, :]), units(ES), every(K_M1), MUL))
                link(nc.gpsimd.tensor_tensor(units(TR[:, :]), units(TR[:, :].bitcast(f32)), every(K_ID), ADD))
            elif name == "lt":
                pool.wait_ge(side_out[1], GDN.after(name, it))
                mask(0)
                link(nc.gpsimd.tensor_tensor(units(UR[:, :]), units(N), every(K_M1T), MUL))
                nc.gpsimd.tensor_tensor(units(UR[:, :]), units(UR[:, :].bitcast(f32)), every(K_ID), ADD)\
                  .then_inc(tu_ready, 1)
                mask(1)
            elif kind == "y" and lv < LEVELS - 2:
                pool.wait_ge(side_full[p], GDN.after(name, it))
                mask(lv + 2)
            elif name == "osum":
                pool.wait_ge(osum_done, g + 1)
                nc.gpsimd.tensor_tensor(ors_c, osum_c, minus_half, ALU.pow).then_inc(ors_done, 1)

        def gdn_pool(pool, link, it):
            which = gdn_which(it)
            for hs in range(32):
                for name, p, w_ in steps_at(GDN_STEPS, hs, which):
                    gdn_step_pool(pool, link, name, p, it - 1 if w_ == SOLVE else it, it)
                if hs == 31 and PREP in which:
                    pool.wait_ge(acc_out[1], GDN.after("z", it))
                    ong = PRM[:, A_ONG:A_ONG + P].unsqueeze(1).broadcast_to([P, 8, P])
                    nc.gpsimd.tensor_tensor(units(zs), units(zs), ong, MUL).then_inc(zg_ready, 1)

        block = ctx.enter_context(nc.Block())

        @block.sync
        def _(sp):
            sp.dma_start(ident, consts[:, 0:P]).then_inc(in_head, 16)
            x_tiles = x.rearrange("(t p) n -> p t n", t=NT)

            def load_x(r):
                cols = slice(r * COLS, (r + 1) * COLS)
                sp.dma_start(H[:, :, cols], x_tiles[:, :, cols]).then_inc(x_in[r], 16)

            def load_chunk(k):
                sp.dma_start(RAW[:, k, :], stream[k]).then_inc(raw_full[k], 16)

            load_x(0)
            sp.dma_start(PRM[:, :], params).then_inc(in_head, 16)
            load_chunk(0)
            load_x(1)
            load_x(2)
            load_chunk(1)
            load_x(3)
            sp.dma_start(K[:, P:], consts[:, P:]).then_inc(in_const, 16)
            sp.dma_start(tailraw, tails[:, 0:KT * 64]).then_inc(tail_in, 16)
            load_chunk(2)
            load_chunk(3)

            def feed(first, end):
                with sp.Fori(first // RAWS, end // RAWS) as i:
                    for k in range(RAWS):
                        sp.wait_ge(lo_ready, i * 2 * RAWS + 2 * (k - RAWS + 1))
                        sp.dma_start(RAW[:, k, :], stream[i * RAWS + k]).then_inc(raw_full[k], 16)

            feed(RAWS, B_KV + 8)
            sp.wait_ge(w_used, 2 * B_KV)
            sp.wait_ge(sumsq, 6)
            sp.dma_start(w2s, w2).then_inc(w2_in, 16)
            sp.dma_start(tailraw2, tails[:, KT * 64:]).then_inc(tail_in, 16)
            feed(B_KV + 8, B_FFN1 + 8)
            sp.wait_ge(w_used, 2 * B_FFN1)
            sp.dma_start(gfs, gfin).then_inc(fin_in, 16)
            feed(B_FFN1 + 8, CHUNKS)
            for t in range(NT):
                sp.wait_ge(y_done, t + 1)
                sp.dma_start(out[t * P:(t + 1) * P, :], hn[:, t, :]).then_inc(out_done, 16)
            sp.wait_ge(out_done, 16 * NT)

        @block.tensor
        def _(pe):
            pe.wait_ge(in_head, 32)
            for r in range(4):
                pe.wait_ge(x_in[r], 16)
                norm_tensor(pe, NORM0, r, None)
            gdn_tensor(pe, 0)
            gdn_tensor(pe, 1)
            with pe.Fori(2, GROUPS) as it:
                gdn_tensor(pe, it)
            gdn_tensor(pe, GROUPS)
            gdn_tensor(pe, GROUPS + 1)
            ffn_tensor(pe, FFN0, B_FFN0, NORM1, 0, None)
            with pe.Fori(1, FBLK) as it:
                ffn_tensor(pe, FFN0, B_FFN0, NORM1, it, None)
            ffn_tensor(pe, FFN0, B_FFN0, NORM1, FBLK, NORM2)
            kv_tensor(pe)
            compress_tensor(pe)
            for r in range(4):
                norm_tensor(pe, NORM3, r, None)
            att_tensor(pe, 0)
            att_tensor(pe, 1)
            with pe.Fori(2, KVG) as it:
                att_tensor(pe, it)
            att_tensor(pe, KVG)
            att_tensor(pe, KVG + 1)
            ffn_tensor(pe, FFN1, B_FFN1, NORM4, 0, None)
            with pe.Fori(1, FBLK) as it:
                ffn_tensor(pe, FFN1, B_FFN1, NORM4, it, None)
            ffn_tensor(pe, FFN1, B_FFN1, NORM4, FBLK, None)

        @block.scalar
        def _(act):
            act.wait_ge(in_head, 32)
            for r in range(4):
                norm_scalar(act, NORM0, 0, r, 0)
                split_hi(act, 0, r)
            for r in range(4):
                act.wait_ge(x_in[r], 16)
            act.wait_ge(in_const, 16)
            squares(act, 0, None, [junk, junk])
            tail_scalar(act, 0, tailraw)
            gdn_scalar(act, 0)
            gdn_scalar(act, 1)
            with act.Fori(2, GROUPS) as it:
                gdn_scalar(act, it)
            gdn_scalar(act, GROUPS)
            gdn_scalar(act, GROUPS + 1)
            ffn_scalar(act, FFN0, B_FFN0, 0, 2, None)
            with act.Fori(1, FBLK) as it:
                ffn_scalar(act, FFN0, B_FFN0, it, 2, None)
            ffn_scalar(act, FFN0, B_FFN0, FBLK, 2, (NORM2, 2, 2))
            kv_scalar(act)
            compress_scalar(act)
            for r in range(4):
                norm_scalar(act, NORM3, 3, r, 3)
            tail_scalar(act, 1, tailraw2)
            att_scalar(act, 0)
            att_scalar(act, 1)
            with act.Fori(2, KVG) as it:
                att_scalar(act, it)
            att_scalar(act, KVG)
            att_scalar(act, KVG + 1)
            ffn_scalar(act, FFN1, B_FFN1, 0, 4, None)
            with act.Fori(1, FBLK) as it:
                ffn_scalar(act, FFN1, B_FFN1, it, 4, None)
            ffn_scalar(act, FFN1, B_FFN1, FBLK, 4, None)
            squares(act, 4, FFN1.end, [hn[:, 0, :], hn[:, 1, :]])

        @block.vector
        def _(dve):
            chain = Chain(dve, dve_chain)
            dve.memset(cin[:, :, 0:3], 0.0).then_inc(pad_zero, 1)
            dve.wait_ge(pad_zero, 1)
            dve.wait_ge(in_head, 32)
            for r in range(4):
                norm_vector(dve, NORM0, 0, r, 0)
                split_lo(dve, 0, r)
            dve.wait_ge(in_const, 16)
            tail_vector(dve, 0, tailraw)
            gdn_vector(dve, chain.link, 0)
            gdn_vector(dve, chain.link, 1)
            chain.loop(2, GROUPS, 16, lambda it: gdn_vector(dve, chain.link, it))
            gdn_vector(dve, chain.link, GROUPS)
            gdn_vector(dve, chain.link, GROUPS + 1)
            ffn_vector(dve, FFN0, B_FFN0, 0, GROUPS, None)
            with dve.Fori(1, FBLK) as it:
                ffn_vector(dve, FFN0, B_FFN0, it, GROUPS, None)
            ffn_vector(dve, FFN0, B_FFN0, FBLK, GROUPS, (NORM2, 2, 2))
            kv_vector(dve)
            compress_vector(dve)
            for r in range(4):
                norm_vector(dve, NORM3, 3, r, 3)
            tail_vector(dve, 1, tailraw2)
            att_vector(dve, chain.link, 0)
            att_vector(dve, chain.link, 1)
            chain.loop(2, KVG, 15, lambda it: att_vector(dve, chain.link, it))
            att_vector(dve, chain.link, KVG)
            att_vector(dve, chain.link, KVG + 1)
            done = GROUPS + FBLK + KVG
            ffn_vector(dve, FFN1, B_FFN1, 0, done, None)
            with dve.Fori(1, FBLK) as it:
                ffn_vector(dve, FFN1, B_FFN1, it, done, None)
            ffn_vector(dve, FFN1, B_FFN1, FBLK, done, None)
            dve.wait_ge(rstd, 5)
            dve.wait_ge(fin_in, 16)
            for t in range(NT):
                nc.vector.scalar_tensor_tensor(hn[:, t, :], H[:, t, :], rstd_c[:, t:t + 1], gfs, MUL, MUL)\
                  .then_inc(y_done, 1)

        @block.gpsimd
        def _(pool):
            chain = Chain(pool, pool_chain)
            pool.wait_ge(in_const, 16)
            rstd_pool(pool, chain.link, 0)
            gdn_pool(pool, chain.link, 0)
            gdn_pool(pool, chain.link, 1)
            chain.loop(2, GROUPS, 5, lambda it: gdn_pool(pool, chain.link, it))
            gdn_pool(pool, chain.link, GROUPS)
            for nth in range(1, 5):
                rstd_pool(pool, chain.link, nth)


def constants():
    import numpy as np
    i = np.arange(P)
    K = np.zeros((P, K_END), np.float32)
    K[:, K_ID:K_ID + P] = i[:, None] == i
    K[:, K_TRI:K_TRI + P] = i[:, None] <= i
    K[:, K_ONE:K_ONE + P] = 1.0
    K[:, K_LOW:K_LOW + P] = i <= i[:, None]
    K[:, K_STR:K_STR + P] = i < i[:, None]
    def couples(r, c, n):
        return (r // (2 * n) == c // (2 * n)) & (r % (2 * n) >= n) & (c % (2 * n) < n)
    K[:, K_M1:K_M1 + P] = -1.0 * couples(i[:, None], i, 1)
    K[:, K_M1T:K_M1T + P] = -1.0 * couples(i, i[:, None], 1)
    for lv in range(LEVELS):
        K[:, K_LV + lv * P:K_LV + (lv + 1) * P] = couples(i, i[:, None], 2 << lv)
    FAR = 1e33
    for t in range(NT):
        tok = (t * P + i)[:, None]
        key = np.arange((t + 1) * P)[None]
        at = K_D0 if t == 0 else K_D1
        K[:, at:at + (t + 1) * P] = np.where(key <= tok, tok - key, FAR)
        n = np.arange(CB)[None]
        ok = 16 * n + CMPB - 1 <= tok
        K[:, K_CD + t * CB:K_CD + (t + 1) * CB] = np.where(ok, tok - (16 * n + (CMPB - 1) / 2), FAR)
        K[:, K_CV + t * CB:K_CV + (t + 1) * CB] = ok
    K[:, K_SL:K_SL + 16] = -(2.0 ** (-8.0 * np.arange(1, 17) / 16))
    K[:, K_EPS] = EPS
    K[:, K_NH:] = -0.5
    return K


def layout(inputs):
    import numpy as np
    f = np.ascontiguousarray

    def chunked(wm, kts, c0):
        return [wm[(k0) * P:(k0 + CHK) * P, c0:c0 + COLS].reshape(CHK, P, COLS).transpose(1, 0, 2).reshape(P, CHUNK)
                for k0 in kts]

    win, wout = inputs["gdn_w_in"][0], inputs["gdn_w_out"][0]
    stream = np.empty((CHUNKS, P, CHUNK), np.float32)
    at = 0

    def put(parts):
        nonlocal at
        for q in parts:
            stream[at] = q
            at += 1

    allk = range(0, KT, CHK)
    QK = 16 * P
    for g in range(GROUPS + 2):
        if g < GROUPS:
            put(chunked(np.concatenate([win[:, 256 * g:256 * g + 256], win[:, QK + 256 * g:QK + 256 * g + 256]], 1), allk, 0))
        if g >= 2:
            for c in range(4):
                put(chunked(wout, [4 * (g - 2)], c * COLS))
        if g < GROUPS:
            put(chunked(win, allk, 2 * QK + COLS * g))
            put(chunked(win, allk, 4 * QK + COLS * g))

    def ffn(l):
        gu, dn = inputs["ffn_w_gate_up"][l], inputs["ffn_w_down"][l]
        for j in range(FBLK + 1):
            if j < FBLK:
                put(chunked(gu, allk, j * COLS))
                put(chunked(gu, allk, FFN_H + j * COLS))
            if j:
                for c in range(4):
                    put(chunked(dn, [4 * (j - 1)], c * COLS))

    ffn(0)
    for c in range(6):
        put(chunked(inputs["kv_w"], allk, c * COLS))
    for wm in (inputs["cmp_w1_k"], inputs["cmp_w1_v"]):
        for c in range(4):
            put([wm[c * 1024:(c + 1) * 1024].reshape(8, P, 256).transpose(1, 0, 2).reshape(P, CHUNK)])
    nin, nout = inputs["nsa_w_in"][0], inputs["nsa_w_out"][0]
    for it in range(KVG + 2):
        if it < KVG:
            put(chunked(nin, allk, it * COLS))
        if it >= 2:
            for c in range(4):
                put(chunked(nout, [4 * (it - 2)], c * COLS))
    ffn(1)
    assert at == CHUNKS

    prm = np.empty((P, A_END), np.float32)
    cw = inputs["gdn_conv_w"][0]
    for g in range(GROUPS):
        for nth in range(2):
            for b in range(4):
                c0 = (256 * g + b * P if b < 2 else QK + 256 * g + (b - 2) * P) if nth == 0 else 2 * QK + COLS * g + b * P
                col = A_CONV + g * 32 + nth * 16 + b * 4
                prm[:, col:col + 4] = cw[:, c0:c0 + P].T
    gains = [inputs["mixer_norm_g"][0], inputs["ffn_norm_g"][0], inputs["kv_norm_g"], inputs["mixer_norm_g"][1],
             inputs["ffn_norm_g"][1]]
    for n, gv in enumerate(gains):
        prm[:, A_GAIN + n * KT:A_GAIN + (n + 1) * KT] = gv.reshape(KT, P).T
    prm[:, A_ALOG:A_ALOG + HEADS] = inputs["gdn_a_log"][0][None]
    prm[:, A_DT:A_DT + HEADS] = inputs["gdn_dt_bias"][0][None]
    prm[:, A_ONG:A_ONG + P] = inputs["gdn_out_norm_g"][0][None]
    prm[:, A_POS:A_POS + CMPB] = inputs["cmp_pos"].T
    tails = np.concatenate([win[:, 6 * QK:].reshape(KT, P, 64).transpose(1, 0, 2).reshape(P, -1),
                            nin[:, 2048:].reshape(KT, P, 48).transpose(1, 0, 2).reshape(P, -1)], 1)
    w2 = np.concatenate([inputs[n].reshape(2, P, P).transpose(1, 0, 2).reshape(P, 256)
                         for n in ("cmp_w2_k", "cmp_w2_v")], 1)
    gfin = np.repeat(inputs["final_norm_g"][None], P, 0)
    return {"stream": stream, "consts": constants(), "params": prm, "tails": f(tails), "w2": f(w2), "gfin": f(gfin),
            "x": f(inputs["x"][0])}


def kernel(**inputs):
    import numpy as np
    import concourse.bacc as bacc
    from concourse.bass_utils import run_bass_kernel_spmd

    arrays = layout({k: np.asarray(v) for k, v in inputs.items()})
    nc = bacc.Bacc("TRN2", target_bir_lowering=False, num_devices=1)
    args = [nc.dram_tensor(k, a.shape, mybir.dt.float32, kind="ExternalInput").ap() for k, a in arrays.items()]
    out = nc.dram_tensor("out", (SEQ, DM), mybir.dt.float32, kind="ExternalOutput").ap()
    build(nc, *args, out)
    r = run_bass_kernel_spmd(nc, [arrays], core_ids=[0])
    return r.results[0]["out"].reshape(1, SEQ, DM)
```
